# Optimizing a Trainium2 kernel written in Bass

```python
import math
import jax, jax.numpy as jnp
from jax import lax
import numpy as np

D_MODEL = 1024
BATCH = 1
SEQ = 512
DEPTH = 2
DEC_BATCH = 8
DEC_SEQ = 4
PAST_LEN = 1024
PAGE_SIZE = 128

N_MIXERS = 2
N_NSA = (DEPTH + 1) // 2
N_ML = DEPTH // 2
NSA_HEADS = 16
NSA_KV_HEADS = 4
NSA_HPG = NSA_HEADS // NSA_KV_HEADS
HEAD_DIM = D_MODEL // NSA_HEADS
CMP_LEN = 32
CMP_STRIDE = 16
CMP_HID = HEAD_DIM
SEL_BLK = 64
SEL_TOPK = 16
WINDOW = 512
Q_BLK = 128
FORCE_BONUS = 1e4
NSA_Q_W = NSA_HEADS * HEAD_DIM
NSA_KV_W = NSA_KV_HEADS * HEAD_DIM
NSA_IN = NSA_Q_W + 6 * NSA_KV_W + 3 * NSA_HEADS
ML_HEADS = 8
ML_DQK = D_MODEL // (2 * ML_HEADS)
ML_DV = D_MODEL // ML_HEADS
ML_CHUNK = 64
ML_QK_W = ML_HEADS * ML_DQK
ML_V_W = ML_HEADS * ML_DV
ML_IN = 2 * ML_QK_W + 2 * ML_V_W + 2 * ML_HEADS
D_FF = 4 * D_MODEL
CONV_W = 3
RMS_EPS = 1e-6
MASK_NEG = -1e30

kernel_name = "nsa_mlstm_hybrid_decode_step"

def rmsnorm(x, g):
    xf = x.astype(jnp.float32)
    y = xf * lax.rsqrt(jnp.mean(xf * xf, axis=-1, keepdims=True) + RMS_EPS)
    return (y * g.astype(jnp.float32)).astype(x.dtype)

def masked_softmax(s, mask):
    s = jnp.where(mask, s.astype(jnp.float32), MASK_NEG)
    e = jnp.exp(s - jnp.max(s, axis=-1, keepdims=True)) * mask
    return e / jnp.maximum(jnp.sum(e, axis=-1, keepdims=True), 1e-30)

def alibi_slopes():
    h = jnp.arange(1, NSA_HEADS + 1, dtype=jnp.float32)
    return jnp.exp2(-8.0 * h / NSA_HEADS).reshape(NSA_KV_HEADS, NSA_HPG)

def nsa_project(h, w_in):
    B, T, _ = h.shape
    p = jnp.einsum('btd,de->bte', h, w_in)
    q = p[..., :NSA_Q_W].reshape(B, T, NSA_KV_HEADS, NSA_HPG, HEAD_DIM)
    kv = p[..., NSA_Q_W:NSA_Q_W + 6 * NSA_KV_W].reshape(B, T, 6, NSA_KV_HEADS, HEAD_DIM)
    gates = p[..., NSA_Q_W + 6 * NSA_KV_W:].reshape(B, T, NSA_KV_HEADS, NSA_HPG, 3)
    return q, kv, gates

def nsa_context(kv, w_cmp1, w_cmp2, cmp_pos):
    B, T = kv.shape[:2]
    ratio = CMP_LEN // CMP_STRIDE
    n_chunk = T // CMP_STRIDE
    nc = n_chunk - ratio + 1
    ch = kv[:, :n_chunk * CMP_STRIDE, :2].reshape(B, n_chunk, CMP_STRIDE, 2, NSA_KV_HEADS, HEAD_DIM)
    pre = None
    for r in range(ratio):
        sl = slice(r * CMP_STRIDE, (r + 1) * CMP_STRIDE)
        part = jnp.einsum('bjlcgd,cldh->bjcgh', ch + cmp_pos[None, None, sl, :, None, :], w_cmp1[:, sl])
        part = part[:, r:r + nc]
        pre = part if pre is None else pre + part
    kvc = jnp.einsum('bjcgh,chd->bjcgd', jax.nn.gelu(pre, approximate=True), w_cmp2)
    kc, vc = kvc[:, :, 0], kvc[:, :, 1]
    c_start = jnp.arange(nc) * CMP_STRIDE
    c_end = c_start + CMP_LEN - 1
    n_sel = -(-T // SEL_BLK)
    sel = jnp.pad(kv[:, :, 2:4], ((0, 0), (0, n_sel * SEL_BLK - T), (0, 0), (0, 0), (0, 0)))
    sel = sel.reshape(B, n_sel, SEL_BLK, 2, NSA_KV_HEADS, HEAD_DIM).transpose(3, 0, 4, 1, 2, 5)
    ks, vs = sel[0], sel[1]
    s_start = jnp.arange(n_sel) * SEL_BLK
    ov = ((c_start[:, None] < s_start[None, :] + SEL_BLK) &
          (c_start[:, None] + CMP_LEN > s_start[None, :])).astype(jnp.float32)
    return kc, vc, c_end, ks, vs, ov

def nsa_core(q, gates, tq, kc, vc, c_end, ks, vs, ov, kw, vw, sw, slopes):
    B, Tq = q.shape[:2]
    scale = HEAD_DIM ** -0.5
    sl5 = slopes[None, :, :, None, None]
    dist_c = tq[:, None] - c_end[None, :]
    sc = jnp.einsum('btghd,bjgd->bghtj', q, kc).astype(jnp.float32) * scale - sl5 * dist_c.astype(jnp.float32)
    pc = masked_softmax(sc, dist_c >= 0)
    oc = jnp.einsum('bghtj,bjgd->btghd', pc.astype(vc.dtype), vc)
    imp = jnp.einsum('bghtj,jn->bgtn', pc, ov)
    n_sel = ks.shape[2]
    bid = jnp.arange(n_sel)
    cur = tq // SEL_BLK
    valid = bid[None, :] * SEL_BLK <= tq[:, None]
    forced = (bid[None, :] == 0) | (bid[None, :] == cur[:, None]) | (bid[None, :] == cur[:, None] - 1)
    score = jnp.where(valid, imp + jnp.where(forced, FORCE_BONUS, 0.0), MASK_NEG)
    k_eff = min(SEL_TOPK, n_sel)
    _, idx = lax.top_k(score, k_eff)
    bi = jnp.arange(B)[:, None, None, None]
    gi = jnp.arange(NSA_KV_HEADS)[None, :, None, None]
    kg = ks[bi, gi, idx].reshape(B, NSA_KV_HEADS, Tq, k_eff * SEL_BLK, HEAD_DIM)
    vg = vs[bi, gi, idx].reshape(B, NSA_KV_HEADS, Tq, k_eff * SEL_BLK, HEAD_DIM)
    s_pos = (idx[..., None] * SEL_BLK + jnp.arange(SEL_BLK)).reshape(B, NSA_KV_HEADS, Tq, k_eff * SEL_BLK)
    dist_s = (tq[None, None, :, None] - s_pos)[:, :, None]
    ss = jnp.einsum('btghd,bgtnd->bghtn', q, kg).astype(jnp.float32) * scale - sl5 * dist_s.astype(jnp.float32)
    ps = masked_softmax(ss, dist_s >= 0)
    osel = jnp.einsum('bghtn,bgtnd->btghd', ps.astype(vg.dtype), vg)
    dist_w = tq[:, None] - sw[None, :]
    swin = jnp.einsum('btghd,bsgd->bghts', q, kw).astype(jnp.float32) * scale - sl5 * dist_w.astype(jnp.float32)
    pw = masked_softmax(swin, (dist_w >= 0) & (dist_w < WINDOW) & (sw[None, :] >= 0))
    ow = jnp.einsum('bghts,bsgd->btghd', pw.astype(vw.dtype), vw)
    g = jax.nn.sigmoid(gates.astype(jnp.float32))
    return g[..., 0:1] * oc + g[..., 1:2] * osel + g[..., 2:3] * ow

def nsa_prompt(h, w_in, w_out, w_cmp1, w_cmp2, cmp_pos, slopes):
    B, T, _ = h.shape
    q, kv, gates = nsa_project(h, w_in)
    kc, vc, c_end, ks, vs, ov = nsa_context(kv[:, :, :4], w_cmp1, w_cmp2, cmp_pos)
    win = kv[:, :, 4:]
    winp = jnp.pad(win, ((0, 0), (WINDOW, 0), (0, 0), (0, 0), (0, 0)))
    qb_len = math.gcd(T, Q_BLK)

    def body(n):
        s0 = n * qb_len
        qb = lax.dynamic_slice_in_dim(q, s0, qb_len, axis=1)
        gb = lax.dynamic_slice_in_dim(gates, s0, qb_len, axis=1)
        wb = lax.dynamic_slice_in_dim(winp, s0, WINDOW + qb_len, axis=1)
        tq = s0 + jnp.arange(qb_len)
        sw = s0 - WINDOW + jnp.arange(WINDOW + qb_len)
        return nsa_core(qb, gb, tq, kc, vc, c_end, ks, vs, ov, wb[:, :, 0], wb[:, :, 1], sw, slopes)

    o = lax.map(body, jnp.arange(T // qb_len))
    o = o.transpose(1, 0, 2, 3, 4, 5).reshape(B, T, NSA_Q_W).astype(h.dtype)
    w_keep = min(WINDOW, T)
    return o @ w_out, kv[:, :, :4], win[:, T - w_keep:]

def nsa_sample(h, cache_kv, page_table, win_buf, w_in, w_out, w_cmp1, w_cmp2, cmp_pos, slopes):
    B, T, _ = h.shape
    q, kv, gates = nsa_project(h, w_in)
    n_pages = page_table.shape[1]
    past_len = n_pages * PAGE_SIZE
    past = cache_kv[page_table].reshape(B, past_len, 4, NSA_KV_HEADS, HEAD_DIM)
    full = jnp.concatenate([past.astype(kv.dtype), kv[:, :, :4]], axis=1)
    kc, vc, c_end, ks, vs, ov = nsa_context(full, w_cmp1, w_cmp2, cmp_pos)
    wfull = jnp.concatenate([win_buf.astype(kv.dtype), kv[:, :, 4:]], axis=1)
    wb_len = win_buf.shape[1]
    sw = past_len - wb_len + jnp.arange(wb_len + T)
    tq = past_len + jnp.arange(T)
    o = nsa_core(q, gates, tq, kc, vc, c_end, ks, vs, ov, wfull[:, :, 0], wfull[:, :, 1], sw, slopes)
    o = o.reshape(B, T, NSA_Q_W).astype(h.dtype)
    return o @ w_out, kv[:, :, :4], wfull[:, T:]

def mlstm_mixer(h, C0, n0, m0, w_in, b_gate, head_norm, w_out):
    B, T, _ = h.shape
    p = jnp.einsum('btd,de->bte', h, w_in)
    f32 = jnp.float32
    q = p[..., :ML_QK_W].reshape(B, T, ML_HEADS, ML_DQK).transpose(0, 2, 1, 3).astype(f32)
    k = p[..., ML_QK_W:2 * ML_QK_W].reshape(B, T, ML_HEADS, ML_DQK).transpose(0, 2, 1, 3).astype(f32) * ML_DQK ** -0.5
    v = p[..., 2 * ML_QK_W:2 * ML_QK_W + ML_V_W].reshape(B, T, ML_HEADS, ML_DV).transpose(0, 2, 1, 3).astype(f32)
    o = p[..., 2 * ML_QK_W + ML_V_W:2 * ML_QK_W + 2 * ML_V_W]
    gp = p[..., 2 * ML_QK_W + 2 * ML_V_W:].reshape(B, T, 2, ML_HEADS).astype(f32) + b_gate.astype(f32)
    ig = gp[:, :, 0].transpose(0, 2, 1)
    logf = jax.nn.log_sigmoid(gp[:, :, 1]).transpose(0, 2, 1)
    L = math.gcd(T, ML_CHUNK)
    nc = T // L

    def chunks(a):
        return jnp.moveaxis(a.reshape(B, ML_HEADS, nc, L, *a.shape[3:]), 2, 0)

    causal = jnp.tril(jnp.ones((L, L), dtype=bool))

    def step(carry, xs):
        C, n, m = carry
        qc, kc, vc, ic, fc = xs
        b = jnp.cumsum(fc, axis=-1)
        D = jnp.where(causal, b[..., :, None] - b[..., None, :] + ic[..., None, :], -jnp.inf)
        inter = b + m[..., None]
        mt = jnp.maximum(inter, jnp.max(D, axis=-1))
        S = jnp.einsum('bhtd,bhsd->bhts', qc, kc) * jnp.exp(D - mt[..., None])
        wi = jnp.exp(inter - mt)
        num = wi[..., None] * jnp.einsum('bhvd,bhtd->bhtv', C, qc) + jnp.einsum('bhts,bhsv->bhtv', S, vc)
        den = wi * jnp.einsum('bhd,bhtd->bht', n, qc) + jnp.sum(S, axis=-1)
        hc = num / jnp.maximum(jnp.abs(den), jnp.exp(-mt))[..., None]
        mL = mt[..., -1]
        decay = jnp.exp(b[..., -1] + m - mL)
        ws = jnp.exp(b[..., -1:] - b + ic - mL[..., None])
        C = decay[..., None, None] * C + jnp.einsum('bhs,bhsv,bhsd->bhvd', ws, vc, kc)
        n = decay[..., None] * n + jnp.einsum('bhs,bhsd->bhd', ws, kc)
        return (C, n, mL), hc

    (C, n, m), hs = lax.scan(step, (C0.astype(f32), n0.astype(f32), m0.astype(f32)),
                             (chunks(q), chunks(k), chunks(v), chunks(ig), chunks(logf)))
    hseq = jnp.moveaxis(hs, 0, 2).reshape(B, ML_HEADS, T, ML_DV).transpose(0, 2, 1, 3)
    hseq = hseq * lax.rsqrt(jnp.mean(hseq * hseq, axis=-1, keepdims=True) + RMS_EPS)
    hseq = hseq.reshape(B, T, ML_V_W) * head_norm.astype(f32) * jax.nn.sigmoid(o.astype(f32))
    return hseq.astype(h.dtype) @ w_out, C, n, m

def conv_ffn(h, buf, w_up, conv_w, conv_b, w_down):
    T = h.shape[1]
    u = h @ w_up
    full = jnp.concatenate([buf.astype(u.dtype), u], axis=1)
    c = conv_b + sum(conv_w[j] * full[:, j:j + T] for j in range(CONV_W))
    y = jax.nn.gelu(c[..., :D_FF], approximate=True) * c[..., D_FF:]
    return y @ w_down, full[:, T:]

def setup_inputs(seed: int = 0) -> dict:
    key = jax.random.key(seed)
    ks = jax.random.split(key, 24)
    n_pages = PAST_LEN // PAGE_SIZE
    n_used = DEC_BATCH * n_pages
    n_phys = n_used + max(1, n_used // 4)
    win_buf = min(WINDOW, PAST_LEN)

    def nrm(k, shape, s=1.0):
        return s * jax.random.normal(k, shape, jnp.float32)

    page_table = jax.random.permutation(ks[8], n_phys)[:n_used].reshape(DEC_BATCH, n_pages).astype(jnp.int32)
    b_gate = jnp.stack([nrm(ks[16], (N_ML, ML_HEADS), 0.1), 3.0 + nrm(ks[17], (N_ML, ML_HEADS), 0.5)], axis=1)
    return {
        "x_prompt": nrm(ks[0], (BATCH, SEQ, D_MODEL)),
        "x_sample": nrm(ks[1], (DEC_BATCH, DEC_SEQ, D_MODEL)),
        "cache_nsa_kv": nrm(ks[2], (N_NSA, n_phys, PAGE_SIZE, 4, NSA_KV_HEADS, HEAD_DIM)),
        "cache_nsa_win": nrm(ks[3], (N_NSA, DEC_BATCH, win_buf, 2, NSA_KV_HEADS, HEAD_DIM)),
        "state_mlstm_C": nrm(ks[4], (N_ML, DEC_BATCH, ML_HEADS, ML_DV, ML_DQK), 0.3),
        "state_mlstm_n": jnp.abs(nrm(ks[5], (N_ML, DEC_BATCH, ML_HEADS, ML_DQK), 0.5)),
        "state_mlstm_m": nrm(ks[6], (N_ML, DEC_BATCH, ML_HEADS)),
        "state_ffn_conv": nrm(ks[7], (DEPTH, DEC_BATCH, CONV_W - 1, 2 * D_FF)),
        "page_table": page_table,
        "norm_g": 1.0 + nrm(ks[9], (DEPTH, 4, D_MODEL), 0.1),
        "w_nsa_in": nrm(ks[10], (N_NSA, D_MODEL, NSA_IN), D_MODEL ** -0.5),
        "w_nsa_out": nrm(ks[11], (N_NSA, NSA_Q_W, D_MODEL), NSA_Q_W ** -0.5),
        "w_cmp1": nrm(ks[12], (N_NSA, 2, CMP_LEN, HEAD_DIM, CMP_HID), (CMP_LEN * HEAD_DIM) ** -0.5),
        "w_cmp2": nrm(ks[13], (N_NSA, 2, CMP_HID, HEAD_DIM), CMP_HID ** -0.5),
        "cmp_pos": nrm(ks[14], (N_NSA, CMP_LEN, 2, HEAD_DIM), 0.5),
        "w_ml_in": nrm(ks[15], (N_ML, D_MODEL, ML_IN), D_MODEL ** -0.5),
        "b_ml_gate": b_gate,
        "ml_head_norm": 1.0 + nrm(ks[18], (N_ML, ML_V_W), 0.1),
        "w_ml_out": nrm(ks[19], (N_ML, ML_V_W, D_MODEL), ML_V_W ** -0.5),
        "w_ffn_up": nrm(ks[20], (DEPTH, D_MODEL, 2 * D_FF), D_MODEL ** -0.5),
        "ffn_conv_w": nrm(ks[21], (DEPTH, CONV_W, 2 * D_FF), CONV_W ** -0.5),
        "ffn_conv_b": nrm(ks[22], (DEPTH, 2 * D_FF), 0.02),
        "w_ffn_down": nrm(ks[23], (DEPTH, D_FF, D_MODEL), D_FF ** -0.5),
    }

def reference(x_prompt, x_sample, cache_nsa_kv, cache_nsa_win, state_mlstm_C, state_mlstm_n, state_mlstm_m,
              state_ffn_conv, page_table, norm_g, w_nsa_in, w_nsa_out, w_cmp1, w_cmp2, cmp_pos, w_ml_in,
              b_ml_gate, ml_head_norm, w_ml_out, w_ffn_up, ffn_conv_w, ffn_conv_b, w_ffn_down):
    slopes = alibi_slopes()
    xp, xs = x_prompt, x_sample
    kv_p, kv_s, win_p, win_s = [], [], [], []
    C_p, C_s, n_p, n_s, m_p, m_s = [], [], [], [], [], []
    cv_p, cv_s = [], []
    for i in range(DEPTH):
        j = i // N_MIXERS
        hp = rmsnorm(xp, norm_g[i, 0])
        hs = rmsnorm(xs, norm_g[i, 0])
        if i % N_MIXERS == 0:
            yp, a, b = nsa_prompt(hp, w_nsa_in[j], w_nsa_out[j], w_cmp1[j], w_cmp2[j], cmp_pos[j], slopes)
            kv_p.append(a); win_p.append(b)
            ys, a, b = nsa_sample(hs, cache_nsa_kv[j], page_table, cache_nsa_win[j], w_nsa_in[j], w_nsa_out[j],
                                  w_cmp1[j], w_cmp2[j], cmp_pos[j], slopes)
            kv_s.append(a); win_s.append(b)
        else:
            Bp = hp.shape[0]
            zC = jnp.zeros((Bp, ML_HEADS, ML_DV, ML_DQK), jnp.float32)
            zn = jnp.zeros((Bp, ML_HEADS, ML_DQK), jnp.float32)
            zm = jnp.zeros((Bp, ML_HEADS), jnp.float32)
            yp, c, n, m = mlstm_mixer(hp, zC, zn, zm, w_ml_in[j], b_ml_gate[j], ml_head_norm[j], w_ml_out[j])
            C_p.append(c); n_p.append(n); m_p.append(m)
            ys, c, n, m = mlstm_mixer(hs, state_mlstm_C[j], state_mlstm_n[j], state_mlstm_m[j], w_ml_in[j],
                                      b_ml_gate[j], ml_head_norm[j], w_ml_out[j])
            C_s.append(c); n_s.append(n); m_s.append(m)
        xp = xp + rmsnorm(yp, norm_g[i, 1])
        xs = xs + rmsnorm(ys, norm_g[i, 1])
        zbuf = jnp.zeros((xp.shape[0], CONV_W - 1, 2 * D_FF), xp.dtype)
        fp, bp = conv_ffn(rmsnorm(xp, norm_g[i, 2]), zbuf, w_ffn_up[i], ffn_conv_w[i], ffn_conv_b[i], w_ffn_down[i])
        fs, bs = conv_ffn(rmsnorm(xs, norm_g[i, 2]), state_ffn_conv[i], w_ffn_up[i], ffn_conv_w[i], ffn_conv_b[i],
                          w_ffn_down[i])
        cv_p.append(bp); cv_s.append(bs)
        xp = xp + rmsnorm(fp, norm_g[i, 3])
        xs = xs + rmsnorm(fs, norm_g[i, 3])
    return (xp, xs, jnp.stack(kv_p), jnp.stack(kv_s), jnp.stack(win_p), jnp.stack(win_s),
            jnp.stack(C_p), jnp.stack(C_s), jnp.stack(n_p), jnp.stack(n_s), jnp.stack(m_p), jnp.stack(m_s),
            jnp.stack(cv_p), jnp.stack(cv_s))


_drawn_inputs = setup_inputs


def setup_inputs(seed=0):
    import zlib

    import numpy as np

    out = dict(_drawn_inputs(seed))
    spreads = {}
    factors = {}
    for name, (base, spread) in spreads.items():
        noise = np.random.default_rng([zlib.crc32(name.encode()), seed]).standard_normal(out[name].shape)
        drawn = base * np.exp(spread * noise) if base else spread * noise
        out[name] = __import__('jax').numpy.asarray(drawn.astype(out[name].dtype))
    for name, factor in factors.items():
        out[name] = (out[name] * factor).astype(out[name].dtype)
    return out
```

```python
from contextlib import ExitStack

import concourse.bass as bass
import numpy as np
from concourse import mybir

F32 = mybir.dt.float32
I32 = mybir.dt.int32
ALU = mybir.AluOpType
ACT = mybir.ActivationFunctionType
AX = mybir.AxisListType.X

P = 128
D = 1024
KT = D // P
SEQ = 512
NB, NS = 8, 4
SMP = NB * NS
T = SEQ + SMP
HALF = T // 2
FF = 4096
DEPTH = 2
EPS = 1e-6
NEG = -1e30
FLOOR = -1e26
PAST = 1024
PAGES, PAGE = 8, 128
HEADS, GROUPS, HPG, HD = 16, 4, 4, 64
ROWS = NS * HEADS
NCMP, NCMP_P = 63, 31
NSEL = 17
WIN = 512
MLH, DQK, DV = 8, 64, 128
TILES = [(i * P, P) for i in range(SEQ // P)] + [(SEQ, SMP)]
KVW = 1536
RING = 4
SLOT = KT * 256



def tables():
    t, at = {}, {}
    t["ident"] = np.eye(P)
    p = np.arange(P)
    dist = p[:, None] + 384 - np.arange(SEQ)[None, :]
    t["negd"] = np.where(dist >= 0, -dist, NEG)
    tq = (np.arange(4)[None, :, None] * P + p[:, None, None]) - (16 * np.arange(NCMP_P) + 31)[None, None, :]
    t["negc"] = np.where(tq >= 0, -tq, NEG).reshape(P, 4 * NCMP_P)
    sl = np.exp2(-8.0 * np.arange(1, HEADS + 1, dtype=np.float32) / HEADS).astype(np.float32)
    order = [(2 * gp + g2) * HPG + h for gp in range(2) for h in range(HPG) for g2 in range(2)]
    t["slopes"] = np.tile(sl[order], (P, 1))
    step, head = np.arange(ROWS) // HEADS, np.arange(ROWS) % HEADS
    pos = PAST + step
    s = sl[head][:, None].astype(np.float32)
    t["s_sel"] = -s * (pos[:, None] - np.arange(PAST)[None, :]).astype(np.float32)
    dw = pos[:, None] - (PAST - WIN + np.arange(WIN))[None, :]
    t["s_win"] = np.where(dw < WIN, -s * dw.astype(np.float32), NEG)
    dn = step[:, None, None] - np.arange(NS)[None, None, :]
    own = np.arange(NB)[:, None, None] == np.arange(NB)[None, :, None]
    new = np.where(dn >= 0, -s[:, :, None] * dn, NEG)[:, None]
    t["s_new"] = np.where(own[None, :, :, :], new[:, :, None, :].reshape(ROWS, 1, 1, NS), NEG).reshape(ROWS, NB * SMP)
    t["s_cmp"] = -s * (pos[:, None] - (16 * np.arange(NCMP) + 31)[None, :]).astype(np.float32)
    t["peers"] = ((step[:, None] == step[None, :]) & (head[:, None] // HPG == head[None, :] // HPG))
    j, n = np.arange(NCMP)[:, None] * 16, np.arange(NSEL)[None, :] * 64
    t["overlap"] = (j < n + 64) & (j + 32 > n)
    blk = np.arange(NSEL)
    t["forced"] = np.tile(np.where((blk == 0) | (blk >= NSEL - 2), 1e4, 0.0), (ROWS, 1))
    t["rank"] = np.tile(blk + 1.0, (ROWS, 1))
    t["causal"] = np.where(p[:, None] <= p[None, :], 0.0, NEG)
    q = np.arange(SMP)
    t["s_causal"] = np.where((q[:, None] // NS == q[None, :] // NS) & (q[:, None] <= q[None, :]), 0.0, NEG)
    t["s_own"] = q[:, None] // NS == np.arange(NB)[None, :]
    width = sum(a.shape[1] for a in t.values())
    out = np.zeros((P, width), np.float32)
    c = 0
    for name, a in t.items():
        at[name] = (c, a.shape[0], a.shape[1])
        out[:a.shape[0], c:c + a.shape[1]] = a
        c += a.shape[1]
    return out, at


class Chain:

    def __init__(self, eng, sem, base=0):
        self.eng, self.sem, self.base, self.k = eng, sem, base, 0

    def link(self, ins):
        self.k += 1
        ins.then_inc(self.sem, 1)
        self.eng.wait_ge(self.sem, self.base + self.k)


M_Q = 0
M_KV = M_Q + 8
M_GATE = M_KV + 15
M_AO = M_GATE + 5
M_UP = [M_AO + 8, 0]
M_DN = [M_UP[0] + 64, 0]
M_MG = M_DN[0] + 16
M_ML = M_MG + 1
M_MV = M_ML + 8
M_MOG = M_MV + 10
M_MO = M_MOG + 8
M_UP[1] = M_MO + 8
M_DN[1] = M_UP[1] + 64

W_Q, W_KV, W_AO = 0, 4, 10
W_ML = W_AO + 4 + 48
W_MO = W_ML + 12
W_UP = [W_AO + 4, W_MO + 4]
W_DN = [W_UP[0] + 32, W_UP[1] + 32]
Q_LOADS, AO_LOADS = 4, 4


def freed(k):
    if k < W_KV:
        return M_Q + 2 * (k + 1)
    if k < W_AO:
        return M_KV + 5 * ((k - W_KV) // 2 + 1)
    if k < W_UP[0]:
        return M_AO + 2 * (k - W_AO + 1)
    if W_DN[0] <= k < W_ML:
        return M_DN[0] + k - W_DN[0] + 1
    if W_ML <= k < W_ML + 4:
        return M_ML + 2 * (k - W_ML + 1)
    if k < W_ML + 8:
        return M_MV + 5 * ((k - W_ML - 4) // 2 + 1)
    if k < W_MO:
        return M_MOG + 2 * (k - W_ML - 8 + 1)
    return M_MO + 2 * (k - W_MO + 1)


def loaded(k):
    return 16 * (k // RING + Q_LOADS + (AO_LOADS - 1 if k >= W_AO else 0))


def trunk(nc, A, O, at, n_const):
    ctx = ExitStack()
    with ctx:
        def sb(name, width, dt=F32, rows=P):
            return ctx.enter_context(nc.sbuf_tensor(name, [rows, width], dt))

        def sem(name):
            return ctx.enter_context(nc.semaphore(name))

        PS = ctx.enter_context(nc.psum_tensor("PS", [P, 8, 512], F32))

        XT = sb("XT", KT * T)[:, :].rearrange("p (k t) -> p k t", k=KT)
        HT = sb("HT", KT * T)[:, :].rearrange("p (k t) -> p k t", k=KT)
        OT = HT
        CONST = sb("CONST", n_const)
        ring = sb("ring", RING * SLOT)
        R = ring[:, :].rearrange("p (s k c) -> p s k c", s=RING, k=KT)
        NG = sb("NG", 64)
        CW = sb("CW", 384)
        CB = sb("CB", 128)
        HN = sb("HN", 8)
        POS = sb("POS", 32)
        WG = sb("WG", KT * 64)[:, :].rearrange("p (k c) -> p k c", k=KT)
        ones = sb("ones", P)
        eps = sb("eps", 1)
        turn = sb("turn", 2)
        RT = sb("RT", T)
        RR = sb("RR", T)
        PT_I = sb("PT_I", PAGES * NB, I32, 1)
        ARENA = 30900
        arena = sb("arena", ARENA)

        def const(name, dims=None, **kw):
            c, rows, n = at[name]
            ap = CONST[0:rows, c:c + n]
            return ap.rearrange(dims, **kw) if dims else ap

        ident = CONST[:, at["ident"][0]:at["ident"][0] + P]

        def area(start):
            place = [start]

            def take(size, dims=None, rows=P, **kw):
                c = place[0]
                place[0] += size
                assert place[0] <= ARENA, place[0]
                ap = arena[0:rows, c:c + size]
                return ap.rearrange(dims, **kw) if dims else ap
            take.place = place
            return take

        ZT = arena[:, ARENA - KT * T:ARENA].rearrange("p (k t) -> p k t", k=KT)
        SQ = arena[:, 0:KT * T].rearrange("p (k t) -> p k t", k=KT)

        a = area(0)
        KVP = a(4 * KVW, "p (i c) -> p i c", i=4)
        KVS = a(KVW)
        QT = a(KT * T, "p (n t) -> p n t", n=KT)
        KTS = a(4 * T, "p (r g t) -> p r g t", r=2, g=2)
        G = a(5 * 48, "p (i c) -> p i c", i=5)
        GS = a(NB * 3, "p (b c) -> p b c", b=NB)
        W1 = a(2 * 8 * P, "p (c a m) -> p c a m", c=2, a=8)
        W2 = a(2 * HD, "p (c d) -> p c d", c=2)
        BP = a(8)
        CJ = a(16 * 256, "p (l c) -> p l c", l=16)
        ct_at = a.place[0]
        CT = a(3 * 512, "p (s g c j) -> p s g c j", s=3, g=4, c=2)
        T1 = a(512, "p (c g j) -> p c g j", c=2, g=4)
        T2 = a(512, "p (c g j) -> p c g j", c=2, g=4)
        GL = a(512, "p (c g j) -> p c g j", c=2, g=4)
        KCT = a(128, "p (g j) -> p g j", g=2)
        VC = a(256)
        scratch_at = a.place[0]
        QS = a(512)
        KCS = a(64)
        VCS = a(128)
        B2 = a(1024, "p (g c) -> p g c", g=2)
        BC = a(248, "p (g i j) -> p g i j", g=2, i=4)
        GH = a(24, "p (i g r) -> p i g r", i=4, g=2)
        SB = a(2 * 512, "p (s c) -> p s c", s=2)
        PB = a(3 * 512, "p (s c) -> p s c", s=3)
        PTS = a(3 * 512, "p (s c) -> p s c", s=3)
        ST = a(4 * 4, "p (s c) -> p s c", s=4)
        b_ = area(ct_at)
        KS = b_(1024, "p (r t) -> p r t", r=2)
        VS = b_(1024, "p (r i c) -> p r i c", r=2, i=4)
        x_ = area(0)
        XR = x_(5 * D, "p (i c) -> p i c", i=5)
        x_ = area(12000)
        RNG, RHN, RPOS = x_(128), x_(128), x_(256)
        RCW, RCB = x_(384, "p (i c) -> p i c", i=3), x_(128)

        f = area(0)
        YT = f(32 * T, "p (k t) -> p k t", k=32)
        U = f(4 * 562, "p (s c) -> p s c", s=4)
        CV = f(4 * 560, "p (s c) -> p s c", s=4)
        UB = f(64 * 16, "p (c r) -> p c r", c=64)
        UL = f(64 * 18, "p (c r) -> p c r", c=64)
        assert f.place[0] <= ARENA - KT * T
        SI = arena[0:16, KT * T:KT * T + 8192]
        SO = arena[0:18, KT * T:KT * T + 8192]
        YR = arena[:, 13000:13000 + 5 * D].rearrange("p (i c) -> p i c", i=5)

        SEL = [ring[:, i * 4096:(i + 1) * 4096].rearrange("p (g c) -> p g c", g=PAGES) for i in range(2)]
        s_ = area(0)
        WB = [s_(2048, "p (i c) -> p i c", i=4) for _ in range(2)]
        KTW = s_(1024, "p (g t) -> p g t", g=2)
        SPT = s_(15 * ROWS, "p (j r) -> p j r", j=15)
        assert s_.place[0] <= 4 * KVW
        s_ = area(scratch_at)
        KTB = s_(2048, "p (g t) -> p g t", g=2)
        SS = SP_ = s_(1664)
        SOA = s_(2 * NB * ROWS, "p (g b r) -> p g b r", g=2, b=NB)
        QB = [s_(2 * ROWS, "p (g r) -> p g r", g=2) for _ in range(2)]
        SST, PCN, AT, NEWB, SE = s_(12), s_(64), s_(64), s_(32), s_(60)

        m_ = area(0)
        QM = m_(4 * T, "p (n t) -> p n t", n=4)
        KM = m_(4 * T, "p (n t) -> p n t", n=4)
        VA = m_(5 * MLH * (DV + 1), "p (i h v) -> p i h v", i=5, h=MLH)
        OS = m_(KT * T, "p (k t) -> p k t", k=KT)
        NUM = m_(2 * MLH * (DV + 1), "p (s h v) -> p s h v", s=2, h=MLH)
        KW = m_(5 * 512, "p (i h d) -> p i h d", i=5, h=MLH)
        SQH = arena[:, m_.place[0]:m_.place[0] + MLH * DV].rearrange("p (h v) -> p h v", h=MLH)
        IG, LF, BB, MS_, R1, C1, WI, EM = (m_(T, rows=MLH) for _ in range(8))
        RD = m_(512, "p (s c) -> p s c", rows=MLH, s=2)
        EX = m_(512, "p (s h t) -> p s h t", s=2, h=2)
        SM = m_(512, "p (s h t) -> p s h t", s=2, h=2)
        TK = m_(120, "p (i q h) -> p i q h", i=5, q=3)
        DCB = m_(96, "p (h g) -> p h g", h=MLH)
        CS = m_(8 * (DV + 1), "p (n g v) -> p n g v", n=4, g=2)
        MST = m_(8 * 8, "p (q h) -> p q h", q=8)
        MP, DC, GB, DCT = m_(12, rows=MLH), m_(12, rows=MLH), m_(2, rows=MLH), m_(8, rows=MLH)
        DD = m_(96, "p (h g) -> p h g", rows=MLH, h=MLH)
        CT0 = m_(MLH * 4 * (DV + 1), "p (h q v) -> p h q v", h=MLH, q=4)
        rg = [0]

        def in_ring(n, rows=P):
            rg[0] += n
            assert rg[0] <= RING * SLOT
            return ring[0:rows, rg[0] - n:rg[0]]

        C0 = in_ring(4096).rearrange("p (h b d) -> p h b d", h=MLH, b=NB)
        QX = in_ring(1024).rearrange("p (h q t) -> p h q t", h=MLH, q=4)
        KB = in_ring(1024).rearrange("p (s b d) -> p s b d", s=2, b=NB)
        NR = in_ring(128, SMP)
        N0 = in_ring(512, NB).rearrange("p (h d) -> p h d", h=MLH)
        EXS = in_ring(256, SMP).rearrange("p (h t) -> p h t", h=MLH)
        SMS = in_ring(256, SMP).rearrange("p (h t) -> p h t", h=MLH)
        CO = KM[:, 0, 0:512].rearrange("p (n g d) -> p n g d", n=4, g=2)

        gsc = nc.dram_tensor("gate_scratch", (SMP, 48), F32, kind="Internal").ap()

        s_x, s_par, s_wg, s_w1, s_pt = sem("s_x"), sem("s_par"), sem("s_wg"), sem("s_w1l"), sem("s_pt")
        s_w = [sem(f"s_ring{i}") for i in range(RING)]
        s_cst, s_xp, s_xe = sem("s_cst"), sem("s_xp"), sem("s_xe")
        s_sq, s_ss, s_rt, s_nrm = sem("s_sq"), sem("s_ss"), sem("s_rt"), sem("s_nrm")
        s_dc, s_gth = sem("s_dc"), sem("s_gth")
        s_mm = sem("s_mm")
        s_qe, s_kve, s_ge, s_tk, s_tke = sem("s_qe"), sem("s_kve"), sem("s_ge"), sem("s_tk"), sem("s_tke")
        s_kvo, s_gso, s_gsi = sem("s_kvo"), sem("s_gso"), sem("s_gsi")
        s_z = sem("s_z")
        s_sil, s_sip, s_sie = sem("s_sil"), sem("s_sip"), sem("s_sie")
        s_ue, s_pad, s_cvd, s_gel, s_y, s_ul = (sem(n) for n in ("s_ue", "s_pad", "s_cvd", "s_gel", "s_y", "s_ul"))
        s_ubw = sem("s_ubw")
        s_mst, s_gte, s_qke, s_ve, s_oe, s_lg, s_row = (
            sem(n) for n in ("s_mst", "s_gte", "s_qke", "s_ve", "s_oe", "s_lg", "s_row"))
        s_rowe, s_tkm, s_tkv, s_ktm, s_kwv, s_rd = (
            sem(n) for n in ("s_rowe", "s_tkm", "s_tkv", "s_ktm", "s_kwv", "s_rd"))
        s_c0, s_c0t, s_c0e, s_n0t, s_qx, s_cth = (sem(n) for n in ("s_c0", "s_c0t", "s_c0e", "s_n0t", "s_qx", "s_cth"))
        s_ma, s_md1, s_mex, s_md2, s_min, s_mi1, s_mit, s_md3, s_md4 = (
            sem(n) for n in ("s_ma", "s_md1", "s_mex", "s_md2", "s_min", "s_mi1", "s_mit", "s_md3", "s_md4"))
        s_ms, s_mrt, s_hv, s_mt, s_mo = (sem(n) for n in ("s_ms", "s_mrt", "s_hv", "s_mt", "s_mo"))
        s_kb, s_cu, s_cn, s_nu, s_nn, s_cst2 = (sem(n) for n in ("s_kb", "s_cu", "s_cn", "s_nu", "s_nn", "s_cst2"))
        s_cp, s_cpe, s_mlo, s_cso = (sem(n) for n in ("s_cp", "s_cpe", "s_mlo", "s_cso"))
        s_kvp, s_cjz, s_cjp, s_cj = sem("s_kvp"), sem("s_cjz"), sem("s_cjp"), sem("s_cj")
        s_sl = [sem("s_sl0"), sem("s_sl1")]
        s_bp, s_bpe, s_ctp, s_cte, s_cm, s_t1, s_t2, s_gl, s_kc, s_kce = (
            sem(n) for n in ("s_bp", "s_bpe", "s_ctp", "s_cte", "s_cm", "s_t1", "s_t2", "s_gl", "s_kc", "s_kce"))
        s_stg, s_qk, s_tt, s_nm, s_ex, s_sc, s_tp, s_te, s_pv, s_ot, s_nc = (
            sem(n) for n in ("s_stg", "s_qk", "s_tt", "s_nm", "s_ex", "s_sc", "s_tp", "s_te", "s_pv", "s_ot", "s_nc"))
        s_qb, s_ktp, s_kte, s_sqk, s_snm, s_sex, s_pcn, s_at, s_ate, s_imp = (
            sem(n) for n in ("s_qb", "s_ktp", "s_kte", "s_sqk", "s_snm", "s_sex", "s_pcn", "s_at", "s_ate", "s_imp"))
        s_ssc, s_stp, s_ste, s_spv, s_so, s_sc2, s_ots = (
            sem(n) for n in ("s_ssc", "s_stp", "s_ste", "s_spv", "s_so", "s_sc2", "s_ots"))
        s_cc = sem("s_cc")
        s_sop, s_soe, s_soo = sem("s_sop"), sem("s_soe"), sem("s_soo")
        s_fp, s_fe, s_fo = sem("s_fp"), sem("s_fe"), sem("s_fo")

        UNITS = [(i, g2, br) for i in (0, 2, 3, 1) for g2 in range(2) for br in range(3)]
        NU = len(UNITS)
        CUTS, ACT_CUTS = (2, 3), (1, 6)
        KC0 = {0: 1600, 1: 0, 2: 1056}

        def unit_width(br, i):
            return NCMP_P if br == 0 else (i + 1) * P

        def turned(a_):
            for l2 in range(2):
                for g2 in range(2):
                    dst = CT[64 * l2:64 * l2 + 64, a_ % 3].rearrange("p g c j -> p g (c j)")[:, g2:4:2, :]
                    src = PS[64 * g2:64 * g2 + 64, a_ % 2, 256 * l2:256 * l2 + 256]
                    yield dst, src.rearrange("p (g x) -> p g x", g=2)

        def nsa_loads(sp):
            sp.wait_ge(s_kvp, 48)
            sp.wait_ge(s_cjz, 1)
            kvo = O["nsa_kv_prompt"].rearrange("n b s c g d -> (n b s) (c g d)")
            for c in range(2):
                sp.dma_start(CJ[64 * c:64 * c + 32, :, :],
                             kvo[:, c * 256:(c + 1) * 256].rearrange("(j l) x -> j l x", l=16)).then_inc(s_cjp, 16)
            cache = A["cache_nsa_kv"].rearrange("n g s c h d -> (n g) s (c h d)")
            win = A["cache_nsa_win"].rearrange("n b (i p) c h d -> (n b) p i (c h d)", p=P)
            sp.wait_ge(s_pt, 16)
            sp.sem_inc(s_spv, 2)
            with sp.Fori(0, NB // 2) as i2:
                for bb in range(2):
                    pages = [sp.value_load(PT_I[0:1, bass.ds(i2 * 16 + (8 * bb + p), 1)], min_val=0, max_val=79)
                             for p in range(PAGES)]
                    sp.wait_ge(s_ctp, i2 * 16 + (8 * bb + 8))
                    for p in range(PAGES):
                        for c in range(2):
                            sp.dma_start(CJ[64 * c + 8 * p:64 * c + 8 * p + 8, :, :],
                                         cache[bass.ds(pages[p], 1), :, c * 256:(c + 1) * 256]
                                         .rearrange("a (j l) x -> (a j) l x", l=16)).then_inc(s_cj, 16)
                    sp.wait_ge(s_mm, M_AO)
                    sp.wait_ge(s_spv, i2 * 2 + (bb + 1))
                    for p in range(PAGES):
                        sp.dma_start(SEL[bb][:, p, :],
                                     cache[bass.ds(pages[p], 1), :, 512:1024].rearrange("a r x -> (a r) x"))\
                            .then_inc(s_sl[bb], 16)
                    sp.wait_ge(s_pv, NU * 8)
                    sp.dma_start(WB[bb], win[bass.ds(i2 * 2 + bb, 1)].rearrange("a p i x -> (a p) i x"))\
                        .then_inc(s_sl[bb], 16)

        def nsa_pe(pe):
            mm, tr = nc.tensor.matmul, nc.tensor.transpose

            def compress(first, e8, e1, ready):
                ready()
                for a_ in range(8):
                    if not (first and a_ < 2):
                        pe.wait_ge(s_cte, e8 + a_ - 1)
                    elif a_ == 0:
                        pe.wait_ge(s_tke, 5)
                    turn_rows(a_)
                    if a_ >= 1:
                        first_layer(e8, a_ - 1)
                first_layer(e8, 7)

            def turn_rows(a_):
                for l2 in range(2):
                    for gp in range(2):
                        q = 2 * l2 + gp
                        last = tr(PS[:, a_ % 2, q * P:(q + 1) * P], CJ[:, 2 * a_ + l2, gp * P:(gp + 1) * P], ident)
                last.then_inc(s_ctp, 1)

            def pause(bank=7):
                mm(PS[0:32, bank, 511:512], ones[:, 0:32], ones[:, 0:1], start=True, stop=True)

            def first_layer(e8, a_):
                pe.wait_ge(s_cte, e8 + a_ + 1)
                for c in range(2):
                    last = mm(PS[:, 2 + c, 0:256], W1[:, c, a_, :], CT[:, a_ % 3, :, c, :],
                              start=(a_ == 0), stop=(a_ == 7))
                last.then_inc(s_cm, 1)

            def second_layer(e1):
                pe.wait_ge(s_gl, e1 + 1)
                pause()
                for g2 in range(2):
                    mm(PS[64 * g2:64 * g2 + 64, 3, 0:2 * NCMP], W2[0:HD, 0, :], GL[0:HD, 0, g2:4:2, 0:NCMP],
                       start=True, stop=True)
                for g in range(4):
                    last = mm(PS[0:NCMP, 3, 128 + g * HD:128 + (g + 1) * HD], GL[0:HD, 1, g, 0:NCMP], W2[0:HD, 1, :],
                              start=True, stop=True)
                last.then_inc(s_kc, 1)

            def prompt_ready():
                pe.wait_ge(s_cjp, 32)
                pe.wait_ge(s_w1, 96)

            pe.wait_ge(s_w1, 96)
            pe.wait_ge(s_tke, 5)
            for c in range(2):
                for a_ in range(8):
                    last = mm(PS[:, 4, 2 * c:2 * c + 2], W1[:, c, a_, :], POS[:, 16 * c + a_:16 * c + 16:8],
                              start=(a_ == 0), stop=(a_ == 7))
            last.then_inc(s_bp, 1)
            compress(True, 0, 0, prompt_ready)
            second_layer(0)
            pe.wait_ge(s_kce, 1)

            with pe.Fori(0, 2) as gp:
                with pe.Fori(0, 4) as h:
                    n24 = gp * (4 * NU) + h * NU
                    pe.wait_ge(s_stg, gp * 8 + h * 2 + 1)

                    def scores(u):
                        i, g2, br = UNITS[u]
                        rows = slice(64 * g2, 64 * g2 + 64)
                        w = unit_width(br, i)
                        if u >= 4:
                            pe.wait_ge(s_tt, n24 + (u - 3))
                        key = KCS[rows, 0:w] if br == 0 else KS[rows, br - 1, 0:w]
                        mm(PS[:, u % 4, 0:w], QS[rows, i * P:(i + 1) * P], key, start=True, stop=True).then_inc(s_qk, 1)

                    def turn_probs(u):
                        i, g2, br = UNITS[u]
                        pe.wait_ge(s_sc, n24 + (u + 1))
                        if u >= 2:
                            pe.wait_ge(s_te, n24 + (u - 1))
                        if br == 0:
                            tr(PS[0:NCMP_P, 4 + u % 2, 0:P], PB[:, u % 3, 0:NCMP_P], ident).then_inc(s_tp, 1)
                        else:
                            for k in range(i + 1):
                                last = tr(PS[:, 4 + u % 2, k * P:(k + 1) * P], PB[:, u % 3, k * P:(k + 1) * P], ident)
                            last.then_inc(s_tp, 1)

                    def values(u):
                        i, g2, br = UNITS[u]
                        pe.wait_ge(s_te, n24 + (u + 1))
                        out = PS[64 * g2:64 * g2 + 64, 6, i * P:(i + 1) * P]
                        cols = slice(64 * g2, 64 * g2 + 64)
                        if u == 0:
                            pe.wait_ge(s_ot, gp * 4 + h + 1)
                        if br == 0:
                            last = mm(out, VCS[0:NCMP_P, cols], PTS[0:NCMP_P, u % 3, 0:P], start=True, stop=False)
                        else:
                            for k in range(i + 1):
                                last = mm(out, VS[:, br - 1, k, cols], PTS[:, u % 3, k * P:(k + 1) * P],
                                          start=False, stop=(br == 2 and k == i))
                        last.then_inc(s_pv, 1)

                    for u in range(NU + 4):
                        if u < NU:
                            scores(u)
                        if 3 <= u < NU + 3:
                            turn_probs(u - 3)
                        if u >= 4:
                            values(u - 4)

            pe.wait_ge(s_ot, 9)
            def first_ready():
                pe.wait_ge(s_cj, 256)
            compress(False, 8, 1, first_ready)

            def sample(i2, bb, more):
                b8 = i2 * 16 + (8 * bb + 8)
                b1 = i2 * 2 + (bb + 1)

                def next_blocks(a0, a1):
                    for a_ in range(a0, a1 if more else a0):
                        if a_ == 0:
                            pe.wait_ge(s_cj, i2 * 512 + 256 * (bb + 2))
                        pe.wait_ge(s_cte, b8 + 8 + a_ - 1)
                        turn_rows(a_)
                        if a_ >= 1:
                            first_layer(b8 + 8, a_ - 1)
                        if a_ == 7:
                            first_layer(b8 + 8, 7)

                pe.wait_ge(s_cte, b8 + 8)
                pe.wait_ge(s_sl[bb], i2 * 144 + 144)
                b6 = i2 * 12 + 6 * bb
                for q in range(6):
                    if q >= 2:
                        pe.wait_ge(s_kte, b6 + (q - 1))
                    for j in range(4):
                        src = (SEL[bb][:, 4 * (q % 2) + j, (q // 2) * P:(q // 2 + 1) * P] if q < 4
                               else WB[bb][:, j, (q - 4) * P:(q - 3) * P])
                        last = tr(PS[:, q % 2, j * P:(j + 1) * P], src, ident)
                    last.then_inc(s_ktp, 1)
                second_layer(b1)
                pe.wait_ge(s_qb, b1)
                pe.wait_ge(s_kte, b6 + 6)
                pe.wait_ge(s_kce, b1 + 1)
                q_ = QB[bb]
                for hf in range(2):
                    for gp in range(2):
                        mm(PS[0:ROWS, 4 + hf, :], q_[:, gp, :], KTB[:, gp, hf * 512:(hf + 1) * 512],
                           start=(gp == 0), stop=(gp == 1))
                for gp in range(2):
                    mm(PS[0:ROWS, 6, :], q_[:, gp, :], KTW[:, gp, :], start=(gp == 0), stop=(gp == 1))
                for r in range(2):
                    for gp in range(2):
                        mm(PS[0:ROWS, 7, 32 * r:32 * r + 32], q_[:, gp, :], KTS[:, r, gp, SEQ:T],
                           start=(gp == 0), stop=(gp == 1))
                for gp in range(2):
                    last = mm(PS[0:ROWS, 7, 64:64 + NCMP], q_[:, gp, :], KCT[:, gp, 0:NCMP],
                              start=(gp == 0), stop=(gp == 1))
                last.then_inc(s_sqk, 1)
                next_blocks(0, CUTS[0])
                pe.wait_ge(s_pcn, b1)
                pause()
                mm(PS[0:NCMP, 7, 128:192], PCN[0:ROWS, 0:NCMP], const("peers"), start=True, stop=True)\
                    .then_inc(s_at, 1)
                next_blocks(CUTS[0], CUTS[1])
                pe.wait_ge(s_ate, b1)
                pause()
                mm(PS[0:ROWS, 7, 192:192 + NSEL], AT[0:NCMP, :], const("overlap"), start=True, stop=True)\
                    .then_inc(s_imp, 1)
                next_blocks(CUTS[1], 8)
                if more:
                    pe.wait_ge(s_cte, b8 + 16)
                pe.wait_ge(s_ssc, i2 * 6 + (3 * bb + 2))
                pause(1)
                for j in range(4):
                    tr(PS[:, 1, j * ROWS:(j + 1) * ROWS], SP_[0:ROWS, 1056 + j * P:1056 + (j + 1) * P],
                       ident[0:ROWS, 0:ROWS])
                tr(PS[0:SMP, 1, 320:384], SP_[0:ROWS, 1568:1600], ident[0:ROWS, 0:ROWS])
                tr(PS[0:NCMP, 1, 384:448], SP_[0:ROWS, 1600:1663], ident[0:ROWS, 0:ROWS]).then_inc(s_stp, 1)
                pe.wait_ge(s_ste, i2 * 4 + (2 * bb + 1))
                for gp in range(2):
                    out = PS[:, 2 + gp, 0:ROWS]
                    vc = slice(256 + gp * P, 256 + (gp + 1) * P)
                    c0 = 1280 + gp * P
                    mm(out, VC[0:NCMP, gp * P:(gp + 1) * P], SPT[0:NCMP, 14, :], start=True, stop=False)
                    for j in range(4):
                        mm(out, WB[bb][:, j, vc], SPT[:, 8 + j, :], start=False, stop=False)
                    mm(out, KVS[0:SMP, c0:c0 + P], SPT[0:SMP, 13, :], start=False, stop=False)
                pe.wait_ge(s_ssc, i2 * 6 + (3 * bb + 3))
                pause(1)
                for j in range(8):
                    tr(PS[:, 0, j * ROWS:(j + 1) * ROWS], SP_[0:ROWS, j * P:(j + 1) * P],
                       ident[0:ROWS, 0:ROWS])
                tr(PS[0:SMP, 1, 256:320], SP_[0:ROWS, 1024:1056], ident[0:ROWS, 0:ROWS]).then_inc(s_stp, 1)
                pe.wait_ge(s_ste, i2 * 4 + (2 * bb + 2))
                for gp in range(2):
                    out = PS[:, 2 + gp, 0:ROWS]
                    vc = slice(256 + gp * P, 256 + (gp + 1) * P)
                    c0 = 768 + gp * P
                    for j in range(8):
                        mm(out, SEL[bb][:, j, vc], SPT[:, j, :], start=False, stop=False)
                    last = mm(out, KVS[0:SMP, c0:c0 + P], SPT[0:SMP, 12, :], start=False, stop=True)
                last.then_inc(s_spv, 1)

            with pe.Fori(0, NB // 2 - 1) as i2:
                for bb in range(2):
                    sample(i2, bb, True)
            for bb in range(2):
                sample(NB // 2 - 1, bb, bb == 0)

        def nsa_act(act):
            copy = nc.scalar.copy

            def compress(first, e8, e1):
                for a_ in range(1, 8, 2):
                    act.wait_ge(s_ctp, e8 + a_ + 1)
                    if not (first and a_ < 3):
                        act.wait_ge(s_cm, e8 + a_ - 2)
                    act.wait_ge(s_cte, e8 + a_)
                    for dst, src in turned(a_):
                        last = copy(dst, src)
                    last.then_inc(s_cte, 1)
                gelu(e1)

            def gelu(e1):
                act.wait_ge(s_t2, e1 + 1)
                for c in range(2):
                    last = nc.scalar.activation(GL[0:HD, c, :, 0:NCMP], T2[0:HD, c, :, 0:NCMP], ACT.Gelu_apprx_tanh,
                                                bias=BP[0:HD, c:c + 1])
                last.then_inc(s_gl, 1)

            act.wait_ge(s_bpe, 1)
            compress(True, 0, 0)
            with act.Fori(0, 2) as gp:
                with act.Fori(0, 4) as h:
                    n24 = gp * (4 * NU) + h * NU
                    for u in range(NU + 3):
                        if u < NU:
                            i, g2, br = UNITS[u]
                            w = unit_width(br, i)
                            if u >= 3:
                                act.wait_ge(s_tp, n24 + (u - 2))
                            act.wait_ge(s_nm, n24 + (u + 1))
                            nc.scalar.activation(PB[:, u % 3, 0:w], SB[:, u % 2, 0:w], ACT.Exp,
                                                 bias=ST[:, u % 4, 1:2], accum_out=ST[:, u % 4, 2:3]).then_inc(s_ex, 1)
                        if u >= 3:
                            e = u - 3
                            i, g2, br = UNITS[e]
                            if e >= 3:
                                act.wait_ge(s_pv, n24 + (e - 2))
                            act.wait_ge(s_tp, n24 + (e + 1))
                            if br == 0:
                                copy(PTS[0:NCMP_P, e % 3, 0:P], PS[0:NCMP_P, 4 + e % 2, 0:P]).then_inc(s_te, 1)
                            else:
                                w = unit_width(br, i)
                                copy(PTS[:, e % 3, 0:w], PS[:, 4 + e % 2, 0:w]).then_inc(s_te, 1)
            compress(False, 8, 1)

            def sample(i2, bb, more):
                b8 = i2 * 16 + (8 * bb + 8)
                b1 = i2 * 2 + (bb + 1)

                def next_chunks(a0, a1):
                    for a_ in range(a0, a1 if more else a0):
                        act.wait_ge(s_ctp, b8 + 8 + a_ + 1)
                        act.wait_ge(s_cm, b8 + 8 + a_ - 2)
                        if a_ == 0:
                            act.wait_ge(s_cte, b8 + 8)
                        for dst, src in turned(a_):
                            last = copy(dst, src)
                        last.then_inc(s_cte, 1)
                b6 = i2 * 12 + 6 * bb
                for q in (1, 3, 5):
                    act.wait_ge(s_ktp, b6 + (q + 1))
                    act.wait_ge(s_kte, b6 + q)
                    dst = KTB[:, q // 2, 512:1024] if q < 4 else KTW[:, 1, :]
                    copy(dst, PS[:, q % 2, :]).then_inc(s_kte, 1)
                for r, br in enumerate((0, 2, 1)):
                    w = (NCMP, 1056, 544)[br]
                    c0 = KC0[br]
                    act.wait_ge(s_snm, i2 * 6 + (3 * bb + r + 1))
                    nc.scalar.activation(SP_[0:ROWS, c0:c0 + w], SS[0:ROWS, c0:c0 + w], ACT.Exp,
                                         bias=SST[0:ROWS, 4 * br + 1:4 * br + 2],
                                         accum_out=SST[0:ROWS, 4 * br + 2:4 * br + 3]).then_inc(s_sex, 1)
                    next_chunks(((0,) + ACT_CUTS)[r], (ACT_CUTS + (8,))[r])
                if more:
                    gelu(b1 + 1)
                act.wait_ge(s_stp, i2 * 4 + (2 * bb + 2))
                act.wait_ge(s_ste, i2 * 4 + (2 * bb + 1))
                copy(SPT[:, 0:8, :].rearrange("p j r -> p (j r)"), PS[:, 0, :])
                copy(SPT[0:SMP, 12, :], PS[0:SMP, 1, 256:320]).then_inc(s_ste, 1)

            with act.Fori(0, NB // 2 - 1) as i2:
                for bb in range(2):
                    sample(i2, bb, True)
            for bb in range(2):
                sample(NB // 2 - 1, bb, bb == 0)

        def nsa_dve(dve, chain):
            v = nc.vector

            def compress(first, e8, e1):
                for a_ in range(0, 8, 2):
                    dve.wait_ge(s_ctp, e8 + a_ + 1)
                    if not (first and a_ < 3):
                        dve.wait_ge(s_cm, e8 + a_ - 2)
                    if not (first and a_ == 0):
                        dve.wait_ge(s_cte, e8 + a_)
                    for dst, src in turned(a_):
                        last = v.tensor_copy(dst, src)
                    last.then_inc(s_cte, 1)
                joined(e8, e1)

            def joined(e8, e1):
                dve.wait_ge(s_cm, e8 + 8)
                for c in range(2):
                    last = v.tensor_copy(T1[0:HD, c, :, 0:NCMP],
                                         PS[HD:P, 2 + c, 0:256].rearrange("p (g j) -> p g j", g=4)[:, :, 1:64])
                last.then_inc(s_t1, 1)
                dve.wait_ge(s_t1, e1 + 1)
                for c in range(2):
                    last = v.tensor_tensor(T2[0:HD, c, :, 0:NCMP],
                                           PS[0:HD, 2 + c, 0:256].rearrange("p (g j) -> p g j", g=4)[:, :, 0:NCMP],
                                           T1[0:HD, c, :, 0:NCMP], ALU.add)
                last.then_inc(s_t2, 1)

            def blocks(e1):
                dve.wait_ge(s_kc, e1 + 1)
                v.tensor_copy(KCT[:, :, 0:NCMP], PS[:, 3, 0:2 * NCMP].rearrange("p (g j) -> p g j", g=2))
                v.tensor_copy(VC[0:NCMP, :], PS[0:NCMP, 3, 128:384]).then_inc(s_kce, 1)

            dve.wait_ge(s_bp, 1)
            chain.link(v.tensor_copy(BP[0:HD, 4:6], PS[HD:P, 4, 1:4:2]))
            v.tensor_tensor(BP[0:HD, 0:2], PS[0:HD, 4, 0:4:2], BP[0:HD, 4:6], ALU.add).then_inc(s_bpe, 1)
            compress(True, 0, 0)
            blocks(0)
            dve.wait_ge(s_ge, 5)
            dve.wait_ge(s_kce, 1)
            slopes = const("slopes")
            def stage(n1, c1):
                v.tensor_copy(QS[:, :], QT[:, bass.ds(n1, 1), 0:SEQ].rearrange("p a t -> p (a t)"))\
                    .then_inc(s_stg, 1)
                for g2 in range(2):
                    sl = slopes[:, bass.ds(n1 * 2 + g2, 1)]
                    v.tensor_scalar(B2[:, g2, :], const("negd"), sl, None, ALU.mult)
                    v.tensor_scalar(BC[:, g2].rearrange("p i j -> p (i j)"), const("negc"), sl, None, ALU.mult)
                    last = v.tensor_copy(GH[:, :, g2, :], G[:, 0:4, bass.ds(c1 + 12 * g2, 3)])
                last.then_inc(s_stg, 1)

            def one_n(gp, h, more):
                n1 = gp * 4 + h
                n24 = gp * (4 * NU) + h * NU
                dve.wait_ge(s_stg, n1 * 2 + 2)
                fc = Chain(dve, s_nc, gp * (4 * (NU + 8)) + h * (NU + 8))

                def biased(u):
                    i, g2, br = UNITS[u]
                    w = unit_width(br, i)
                    if u >= 2:
                        dve.wait_ge(s_ex, n24 + (u - 1))
                    dve.wait_ge(s_qk, n24 + (u + 1))
                    v.memset(turn[0:1, 0:1], 0.0)
                    bias = BC[:, g2, i, :] if br == 0 else B2[:, g2, (3 - i) * P:512]
                    v.tensor_tensor_reduce(out=SB[:, u % 2, 0:w], in0=PS[:, u % 4, 0:w], in1=bias, scale=1.0,
                                           scalar=NEG, op0=ALU.add, op1=ALU.max,
                                           accum_out=ST[:, u % 4, 0:1]).then_inc(s_tt, 1)
                    dve.wait_ge(s_tt, n24 + (u + 1))
                    v.tensor_scalar(ST[:, u % 4, 1:2], ST[:, u % 4, 0:1], FLOOR, -1.0, ALU.max, ALU.mult)\
                        .then_inc(s_nm, 1)

                def weighed(u):
                    i, g2, br = UNITS[u]
                    w = unit_width(br, i)
                    st = ST[:, u % 4, :]
                    dve.wait_ge(s_ex, n24 + (u + 1))
                    if br == 0:
                        fc.link(v.tensor_scalar(st[:, 2:3], st[:, 2:3], 1e-30, None, ALU.max))
                    fc.link(v.reciprocal(st[:, 3:4], st[:, 2:3]))
                    v.tensor_scalar(PB[:, u % 3, 0:w], PB[:, u % 3, 0:w], st[:, 3:4],
                                    GH[:, i, g2, br:br + 1], ALU.mult, ALU.mult).then_inc(s_sc, 1)

                for u in range(NU + 2):
                    if u < NU:
                        biased(u)
                    if u >= 2:
                        weighed(u - 2)
                assert fc.k == NU + 8
                if more:
                    dve.wait_ge(s_sc, n24 + NU)
                    stage(n1 + 1, gp * 24 + h * 3 + 3)
                dve.wait_ge(s_pv, n24 + NU)
                v.tensor_copy(OT[:, bass.ds(n1, 1), 0:SEQ].rearrange("p a t -> p (a t)"), PS[:, 6, :])\
                    .then_inc(s_ot, 1)

            v.memset(turn[0:1, 0:1], 0.0).then_inc(s_ot, 1)
            with dve.Fori(0, 2) as gp:
                for r in range(2):
                    v.tensor_copy(KS[:, r, :], KTS[:, r, bass.ds(gp, 1), 0:SEQ].rearrange("p a t -> p (a t)"))
                    v.tensor_copy(VS[:, r], KVP[:, :, bass.ds(gp * P + (768 + 512 * r), P)])
                v.tensor_copy(KCS[:, 0:NCMP_P], KCT[:, bass.ds(gp, 1), 0:NCMP_P].rearrange("p a t -> p (a t)"))
                v.tensor_copy(VCS[0:NCMP_P, :], VC[0:NCMP_P, bass.ds(gp * P, P)])
                stage(gp * 4, gp * 24)
                with dve.Fori(0, 3) as h:
                    one_n(gp, h, True)
                one_n(gp, 3, False)

            for bb in range(2):
                chain.link(v.memset(QB[bb], 0.0))
            dve.wait_ge(s_gsi, 64)
            compress(False, 8, 1)

            def sample(i2, bb, more):
                b8 = i2 * 16 + (8 * bb + 8)
                b1 = i2 * 2 + (bb + 1)
                b6 = i2 * 12 + 6 * bb
                SC_N = 20
                fc = Chain(dve, s_sc2, i2 * (2 * SC_N) + bb * SC_N)
                for gp in range(2):
                    for g2 in range(2):
                        g = 2 * gp + g2
                        dst = QB[bb][64 * g2:64 * g2 + 64, gp, :].rearrange("p (s g h) -> p g h s", s=NS, g=4)[:, g]
                        last = v.tensor_copy(dst, QT[64 * g2:64 * g2 + 64, 4 * gp:4 * gp + 4,
                                                     bass.ds(i2 * 8 + (SEQ + 4 * bb), 4)])
                last.then_inc(s_qb, 1)
                for q in (0, 2, 4):
                    dve.wait_ge(s_ktp, b6 + (q + 1))
                    if q:
                        dve.wait_ge(s_kte, b6 + q)
                    dst = KTB[:, q // 2, 0:512] if q < 4 else KTW[:, 0, :]
                    v.tensor_copy(dst, PS[:, q % 2, :]).then_inc(s_kte, 1)
                blocks(b1)
                dve.wait_ge(s_sqk, b1)
                new = const("s_new")[:, bass.ds(i2 * 64 + 32 * bb, 32)]
                chain_st = {br: SST[0:ROWS, 4 * br:4 * br + 4] for br in range(3)}

                def floor(br):
                    st = chain_st[br]
                    v.tensor_scalar(st[:, 1:2], st[:, 0:1], FLOOR, -1.0, ALU.max, ALU.mult).then_inc(s_snm, 1)

                def ttr(c0, w, psum, bias, init, br):
                    fc.link(v.tensor_tensor_reduce(out=SS[0:ROWS, c0:c0 + w], in0=psum, in1=bias, scale=1.0,
                                                   scalar=init, op0=ALU.add, op1=ALU.max,
                                                   accum_out=chain_st[br][:, 0:1]))
                v.memset(turn[0:1, 0:1], 0.0)
                ttr(1600, NCMP, PS[0:ROWS, 7, 64:64 + NCMP], const("s_cmp"), NEG, 0)
                floor(0)
                fc.link(v.tensor_copy(NEWB[0:ROWS, :], new))
                v.memset(turn[0:1, 0:1], 0.0)
                ttr(1056, WIN, PS[0:ROWS, 6, :], const("s_win"), NEG, 2)
                fc.link(v.memset(turn[0:1, 0:1], 0.0))
                v.memset(turn[0:1, 0:1], 0.0)
                ttr(1568, SMP, PS[0:ROWS, 7, 32:64], NEWB[0:ROWS, :], chain_st[2][:, 0:1], 2)
                floor(2)
                dve.wait_ge(s_sex, i2 * 6 + (3 * bb + 1))
                st = chain_st[0]
                fc.link(v.tensor_scalar(st[:, 2:3], st[:, 2:3], 1e-30, None, ALU.max))
                fc.link(v.reciprocal(st[:, 3:4], st[:, 2:3]))
                v.tensor_scalar(PCN[0:ROWS, 0:NCMP], SP_[0:ROWS, 1600:1663], st[:, 3:4], None, ALU.mult)\
                    .then_inc(s_pcn, 1)
                dve.wait_ge(s_pcn, b1)
                gate = [GS[0:ROWS, bass.ds(i2 * 2 + bb, 1), r:r + 1].rearrange("p a r -> p (a r)") for r in range(3)]
                v.tensor_scalar(SP_[0:ROWS, 1600:1663], PCN[0:ROWS, 0:NCMP], gate[0], None, ALU.mult)\
                    .then_inc(s_ssc, 1)
                dve.wait_ge(s_at, b1)
                v.tensor_copy(AT[0:NCMP, :], PS[0:NCMP, 7, 128:192]).then_inc(s_ate, 1)

                def share(r, br):
                    w, c0 = (0, 1056, 544)[br], KC0[br]
                    st = chain_st[br]
                    dve.wait_ge(s_sex, i2 * 6 + (3 * bb + 2 + r))
                    fc.link(v.reciprocal(st[:, 3:4], st[:, 2:3]))
                    v.tensor_scalar(SP_[0:ROWS, c0:c0 + w], SP_[0:ROWS, c0:c0 + w], st[:, 3:4], gate[br],
                                    ALU.mult, ALU.mult).then_inc(s_ssc, 1)
                share(0, 2)
                dve.wait_ge(s_imp, b1)
                fc.link(v.tensor_tensor(SE[0:ROWS, 0:17], PS[0:ROWS, 7, 192:209], const("forced"), ALU.add))
                fc.link(v.tensor_reduce(SE[0:ROWS, 17:18], SE[0:ROWS, 0:17], AX, ALU.min))
                fc.link(v.scalar_tensor_tensor(out=SE[0:ROWS, 20:37], in0=SE[0:ROWS, 0:17],
                                               scalar=SE[0:ROWS, 17:18], in1=const("rank"),
                                               op0=ALU.is_le, op1=ALU.mult))
                fc.link(v.tensor_reduce(SE[0:ROWS, 18:19], SE[0:ROWS, 20:37], AX, ALU.max))
                fc.link(v.tensor_scalar(SE[0:ROWS, 40:57], SE[0:ROWS, 20:37], SE[0:ROWS, 18:19], NEG,
                                        ALU.is_equal, ALU.mult))
                fc.link(v.tensor_tensor(SS[0:ROWS, 0:1024].rearrange("p (n k) -> p n k", n=16),
                                        const("s_sel").rearrange("p (n k) -> p n k", n=16),
                                        SE[0:ROWS, 40:56].unsqueeze(2).to_broadcast([ROWS, 16, 64]), ALU.add))
                v.memset(turn[0:1, 0:1], 0.0)
                ttr(0, PAST, PS[0:ROWS, 4:6, :].rearrange("p a c -> p (a c)"), SS[0:ROWS, 0:1024], NEG, 1)
                v.memset(turn[0:1, 0:1], 0.0)
                ttr(1024, SMP, PS[0:ROWS, 7, 0:32], NEWB[0:ROWS, :], chain_st[1][:, 0:1], 1)
                floor(1)
                if more:
                    joined(b8 + 8, b1 + 1)
                dve.wait_ge(s_stp, i2 * 4 + (2 * bb + 1))
                v.tensor_copy(SPT[:, 8:12, :].rearrange("p j r -> p (j r)"), PS[:, 1, 0:256])
                v.tensor_copy(SPT[0:SMP, 13, :], PS[0:SMP, 1, 320:384])
                v.tensor_copy(SPT[0:NCMP, 14, :], PS[0:NCMP, 1, 384:448]).then_inc(s_ste, 1)
                share(1, 1)
                assert fc.k <= SC_N, fc.k
                while fc.k < SC_N:
                    fc.link(v.memset(turn[0:1, 0:1], 0.0))
                dve.wait_ge(s_spv, b1 + 2)
                v.tensor_copy(SOA[:, :, bass.ds(i2 * 2 + bb, 1), :].rearrange("p g a r -> p g (a r)"),
                              PS[:, 2:4, 0:ROWS]).then_inc(s_so, 1)

            with dve.Fori(0, NB // 2 - 1) as i2:
                for bb in range(2):
                    sample(i2, bb, True)
            for bb in range(2):
                sample(NB // 2 - 1, bb, bb == 0)
            dve.wait_ge(s_so, 8)
            for gp in range(2):
                for g2 in range(2):
                    g = 2 * gp + g2
                    rows = slice(64 * g2, 64 * g2 + 64)
                    for h in range(HPG):
                        v.tensor_copy(OT[rows, 4 * gp + h, SEQ:T].rearrange("p (b s) -> p b s", b=NB),
                                      SOA[rows, gp].rearrange("p b (s c) -> p b s c", s=NS)[:, :, :, 4 * g + h])\
                            .then_inc(s_ots, 1)


        ML_READY = ((s_mo, 40), (s_cpe, 1))
        INTER = [(6, 0), (6, 1), (6, 2), (7, 0), (7, 1), (7, 2), (2, 0), (2, 1)]
        INTRA = [(3, 0), (3, 1), (3, 2), (5, 0), (5, 1), (5, 2), (4, 0), (4, 1)]
        W129 = DV + 1

        def ml_loads(sp, slot):
            sp.wait_ge(s_soo, 32)
            with nc.allow_non_contiguous_dma(reason="80 gate biases and maxima change places"):
                sp.dma_start(GB, A["b_ml_gate"][0].rearrange("g h -> h g")).then_inc(s_mst, 16)
                sp.dma_start(MP[:, 4:12], A["state_mlstm_m"][0].rearrange("b h -> h b")).then_inc(s_mst, 16)
            for k in range(12):
                slot(W_ML + k, w_ml[:, :, k * 256:(k + 1) * 256])
            sp.wait_ge(s_mm, M_MOG + 8)
            for h in range(MLH):
                sp.dma_start(C0[:, h], A["state_mlstm_C"][0, :, h].rearrange("b v d -> v b d")).then_inc(s_c0, 16)
            for q in range(4):
                sp.dma_start(NR[8 * q:8 * q + 8, :].rearrange("h (b d) -> h b d", b=2),
                             A["state_mlstm_n"][0, 2 * q:2 * q + 2].rearrange("b h d -> h b d")).then_inc(s_c0, 16)
            sp.dma_start(N0.rearrange("b h d -> b (h d)"), A["state_mlstm_n"][0].rearrange("b h d -> b (h d)"))\
                .then_inc(s_c0, 16)
            sp.wait_ge(s_cso, 16 * (MLH + 1))
            sp.wait_ge(s_mt, 1)
            sp.wait_ge(s_cu, MLH)

        def ml_pe(pe):
            mm, tr = nc.tensor.matmul, nc.tensor.transpose

            pe.wait_ge(s_wg, 32)
            pe.wait_ge(s_soe, 16)
            for g in range(2):
                for k in range(KT):
                    if g == 0:
                        pe.wait_ge(s_nrm, 32 + k + 1)
                    for hf in range(2):
                        last = mm(PS[0:MLH, 2 * g + hf, 0:HALF], WG[:, k, 48 + 8 * g:56 + 8 * g],
                                  HT[:, k, hf * HALF:(hf + 1) * HALF], start=(k == 0), stop=(k == KT - 1))
            last.then_inc(s_mm, 1)

            def chunk(bank, r, mc):
                for k in range(KT):
                    for hf in range(2):
                        last = mm(PS[:, bank + hf, 0:HALF], R[:, r, k, mc * P:(mc + 1) * P],
                                  HT[:, k, hf * HALF:(hf + 1) * HALF], start=(k == 0), stop=(k == KT - 1))
                return last

            for n in range(8):
                k0 = W_ML + n // 2
                if n % 2 == 0:
                    pe.wait_ge(s_w[k0 % RING], loaded(k0))
                if n >= 2:
                    pe.wait_ge(s_qke, n - 1)
                chunk(4 + 2 * (n % 2), k0 % RING, n % 2).then_inc(s_mm, 1)
            pe.wait_ge(s_gte, 2)
            for m in range(10):
                pr, i = divmod(m, 5)
                k0 = W_ML + 4 + 2 * pr
                if i == 0:
                    for s in range(2):
                        pe.wait_ge(s_w[(k0 + s) % RING], loaded(k0 + s))
                if m >= 4:
                    pe.wait_ge(s_ve, m - 3)
                t0, rows = TILES[i]
                r0 = k0 % RING
                for k in range(KT):
                    last = mm(PS[0:rows, m % 4, :], HT[:, k, t0:t0 + rows], R[:, r0:r0 + 2, k, :],
                              start=(k == 0), stop=(k == KT - 1))
                last.then_inc(s_mm, 1)
            pe.wait_ge(s_qke, 8)
            for n in range(8):
                k0 = W_ML + 8 + n // 2
                if n % 2 == 0:
                    pe.wait_ge(s_w[k0 % RING], loaded(k0))
                if n >= 2:
                    pe.wait_ge(s_oe, n - 1)
                chunk(4 + 2 * (n % 2), k0 % RING, n % 2).then_inc(s_mm, 1)

            pe.wait_ge(s_ve, 10)
            pe.wait_ge(s_rowe, 4)
            for i, (t0, rows) in enumerate(TILES):
                for q, row in enumerate((WI, EM, LF)):
                    tr(PS[0:rows, 0, 24 * i + 8 * q:24 * i + 8 * q + 8], row[:, t0:t0 + rows], ident[0:8, 0:8])
            tr(PS[0:NB, 1, 128:136], DC[:, 4:12], ident[0:8, 0:8])
            pe.wait_ge(s_cst2, 1)
            mm(PS[:, 1, 0:96], ones[0:MLH, :], DD.rearrange("p h g -> p (h g)"), start=True, stop=True)\
                .then_inc(s_tkm, 1)
            for i, (t0, rows) in enumerate(TILES):
                if i >= 2:
                    pe.wait_ge(s_kwv, i - 1)
                for n in range(4):
                    last = tr(PS[0:rows, 2 + i % 2, n * P:(n + 1) * P], KM[:, n, t0:t0 + rows], ident)
                last.then_inc(s_ktm, 1)

            pe.wait_ge(s_oe, 8)
            pe.wait_ge(s_rd, 1)
            col = slice(SEQ, T)
            idn = ident[0:8, 0:8]
            mm(PS[0:SMP, 4, 0:256], ones[0:MLH, 0:SMP], RD[:, 0, :], start=True, stop=False)
            mm(PS[0:SMP, 4, 0:256], C1[:, col], idn.unsqueeze(2).to_broadcast([8, 8, SMP]), start=False, stop=True)
            for h in range(MLH):
                rows = slice(64 * (h % 2), 64 * (h % 2) + 64)
                last = mm(PS[0:SMP, 4 + h % 2, 256 + 32 * (h // 2):288 + 32 * (h // 2)], KM[rows, h // 2, col],
                          QM[rows, h // 2, col], start=True, stop=True)
            last.then_inc(s_ma, 1)
            pe.wait_ge(s_c0, 16 * (MLH + 5))
            pe.wait_ge(s_tkv, 1)
            pe.wait_ge(s_kwv, 5)
            tr(PS[:, 3, 0:32], NR, ident[0:32, 0:32]).then_inc(s_n0t, 1)
            for h in range(MLH):
                if h >= 2:
                    pe.wait_ge(s_c0e, h - 1)
                for q in range(4):
                    last = tr(PS[:, h % 2, q * P:(q + 1) * P],
                              C0[:, h, 2 * q:2 * q + 2, :].rearrange("p b d -> p (b d)"), ident)
                last.then_inc(s_c0t, 1)
            pe.wait_ge(s_qx, 1)
            pe.wait_ge(s_kwv, 5)
            pe.wait_ge(s_c0e, MLH)
            for h, (bank, j) in enumerate(INTER):
                for q in range(4):
                    last = mm(PS[0:SMP, bank, j * W129:(j + 1) * W129], QX[:, h, q, :], CT0[:, h, q, :],
                              start=(q == 0), stop=(q == 3))
            last.then_inc(s_min, 1)
            pe.wait_ge(s_md2, 1)
            for h, (bank, j) in enumerate(INTRA):
                last = mm(PS[0:SMP, bank, j * W129:(j + 1) * W129], SMS[:, h, :], VA[0:SMP, 4, h, :],
                          start=True, stop=True)
            last.then_inc(s_mit, 1)
            for h in range(MLH):
                pe.wait_ge(s_kb, h + 1)
                if h >= 2:
                    pe.wait_ge(s_cn, h - 1)
                mm(PS[:, h % 2, :], VA[0:SMP, 4, h, 0:DV], KB[0:SMP, h % 2].rearrange("p b d -> p (b d)"),
                   start=True, stop=True).then_inc(s_cu, 1)
            pe.wait_ge(s_mi1, 1)
            mm(PS[0:NB, 2, :], const("s_own"), KW[0:SMP, 4].rearrange("p h d -> p (h d)"), start=True, stop=True)\
                .then_inc(s_nu, 1)

            def turn_tile(j):
                i = 4 if j == 0 else j - 1
                rows = TILES[i][1]
                pe.wait_ge(s_hv, j + 1)
                if j:
                    pe.wait_ge(s_mo, 8 * j)
                for h in range(MLH):
                    last = tr(PS[:, 6 + h // 4, (h % 4) * P:(h % 4) * P + rows], NUM[0:rows, j % 2, h, 0:DV],
                              ident[0:rows, 0:rows])
                last.then_inc(s_mt, 1)

            turn_tile(0)
            pe.wait_ge(s_nn, 1)
            pe.wait_ge(s_cn, MLH)

            def intra(u):
                c, n = divmod(u, 4)
                pe.wait_ge(s_md2, u + 2)
                if u >= 2:
                    pe.wait_ge(s_md3, u)
                elif u == 0:
                    pe.wait_ge(s_md3, 1)
                for h2 in range(2):
                    last = mm(PS[:, 4 + u % 2, h2 * W129:(h2 + 1) * W129], SM[:, u % 2, h2, :],
                              VA[:, c, 2 * n + h2, :], start=True, stop=True)
                last.then_inc(s_mit, 1)

            for u in range(16):
                c, n = divmod(u, 4)
                toks = slice(c * P, (c + 1) * P)
                pe.wait_ge(s_rd, u + 2)
                if u >= 2:
                    pe.wait_ge(s_md2, u)
                    pe.wait_ge(s_md3, u)
                else:
                    pe.wait_ge(s_md3, 1)
                mm(PS[:, u % 2, 0:256], ones[0:MLH, :], RD[:, (u + 1) % 2, :], start=True, stop=False)
                mm(PS[:, u % 2, 0:256], C1[:, toks], idn[:, 2 * n:2 * n + 2].unsqueeze(2).to_broadcast([8, 2, P]),
                   start=False, stop=True)
                for h2 in range(2):
                    rows = slice(64 * h2, 64 * h2 + 64)
                    bank, c0 = ((u % 2, 256), (4 + u % 2, 384))[h2]
                    last = mm(PS[:, bank, c0:c0 + P], KM[rows, n, toks], QM[rows, n, toks], start=True, stop=True)
                last.then_inc(s_ma, 1)
                if u >= 2:
                    pe.wait_ge(s_mi1, u)
                    pe.wait_ge(s_md4, u - 1)
                if c:
                    pe.wait_ge(s_md4, u - 3)
                    mm(PS[:, 2 + u % 2, 0:2 * W129], QM[:, n, toks], CS[:, n, :, :], start=True, stop=True)
                for h2 in range(2):
                    last = mm(PS[64 * h2:64 * h2 + 64, 2 + u % 2, 260:260 + W129], KW[:, c, 2 * n + h2, :],
                              VA[:, c, 2 * n + h2, :], start=True, stop=True)
                last.then_inc(s_min, 1)
                if u >= 1:
                    intra(u - 1)
                if u % 4 == 2 and c:
                    turn_tile(c)
            intra(15)
            turn_tile(4)
            pe.wait_ge(s_md4, 16)
            for h2 in range(2):
                rows = slice(64 * h2, 64 * h2 + 64)
                for n in range(4):
                    last = tr(PS[:, h2, n * DQK:(n + 1) * DQK], CS[rows, n, h2, 0:DV], ident[rows, rows])
            last.then_inc(s_cp, 1)

        def ml_act(act):
            copy = nc.scalar.copy
            act.wait_ge(s_soo, 32)
            act.wait_ge(s_mst, 32)
            act.wait_ge(s_mm, M_MG + 1)
            for g, row in enumerate((IG, LF)):
                nc.scalar.activation(halves(row), PS[0:MLH, 2 * g:2 * g + 2, 0:HALF], ACT.Identity,
                                     bias=GB[:, g:g + 1]).then_inc(s_gte, 1)
            act.wait_ge(s_gte, 2)
            nc.scalar.activation(R1, LF, ACT.Abs).then_inc(s_lg, 1)
            act.wait_ge(s_lg, 1)
            nc.scalar.activation(R1, R1, ACT.Exp, scale=-1.0).then_inc(s_lg, 1)
            act.wait_ge(s_lg, 2)
            nc.scalar.activation(R1, R1, ACT.Ln, bias=ones[0:MLH, 0:1]).then_inc(s_lg, 1)
            for n in range(8):
                act.wait_ge(s_mm, M_ML + n + 1)
                dst = (QM if n < 4 else KM)[:, n % 4, :]
                src = PS[:, 4 + 2 * (n % 2):6 + 2 * (n % 2), 0:HALF]
                nc.scalar.activation(halves(dst), src, ACT.Copy, scale=1.0 if n < 4 else DQK ** -0.5).then_inc(s_qke, 1)
            act.wait_ge(s_row, 1)
            nc.scalar.activation(WI, WI, ACT.Exp).then_inc(s_rowe, 1)
            nc.scalar.activation(EM, MS_, ACT.Exp, scale=-1.0).then_inc(s_rowe, 1)
            nc.scalar.activation(LF, LF, ACT.Exp).then_inc(s_rowe, 1)
            nc.scalar.activation(DC, DC, ACT.Exp).then_inc(s_rowe, 1)
            for n in range(8):
                act.wait_ge(s_mm, M_MOG + n + 1)
                src = PS[:, 4 + 2 * (n % 2):6 + 2 * (n % 2), 0:HALF]
                nc.scalar.activation(halves(OS[:, n, :]), src, ACT.Sigmoid).then_inc(s_oe, 1)
            act.wait_ge(s_n0t, 1)
            copy(CT0[:, :, :, DV].rearrange("p h q -> p q h"),
                 PS[:, 3, 0:32].rearrange("p (q h) -> p q h", q=4))
            for h in range(MLH):
                act.wait_ge(s_c0t, h + 1)
                copy(CT0[:, h, :, 0:DV], PS[:, h % 2, :].rearrange("p (q v) -> p q v", q=4)).then_inc(s_c0e, 1)
            act.wait_ge(s_md1, 1)
            nc.scalar.activation(EXS, EXS, ACT.Exp).then_inc(s_mex, 1)
            act.wait_ge(s_min, 1)
            act.wait_ge(s_tkv, 2)
            for h, (bank, j) in enumerate(INTER):
                last = nc.scalar.activation(NUM[0:SMP, 0, h, :], PS[0:SMP, bank, j * W129:(j + 1) * W129], ACT.Copy,
                                            scale=TK[0:SMP, 4, 0, h:h + 1])
            last.then_inc(s_mi1, 1)

            def root(j):
                rows = SMP if j == 0 else P
                act.wait_ge(s_ms, j + 1)
                nc.scalar.activation(MST[0:rows, 4, :], MST[0:rows, 3, :], ACT.Sqrt, bias=eps[0:rows, 0:1],
                                     scale=1.0 / DV).then_inc(s_mrt, 1)

            root(0)
            for u in range(16):
                c, n = divmod(u, 4)
                act.wait_ge(s_md1, u + 2)
                nc.scalar.activation(EX[:, u % 2], EX[:, u % 2], ACT.Exp).then_inc(s_mex, 1)
                act.wait_ge(s_min, u + 2)
                if c:
                    act.wait_ge(s_mt, c)
                    act.wait_ge(s_md4, u + 1)
                    for h2 in range(2):
                        last = nc.scalar.activation(NUM[:, (c + 1) % 2, 2 * n + h2, :],
                                                    PS[:, 2 + u % 2, h2 * W129:(h2 + 1) * W129], ACT.Copy,
                                                    scale=TK[:, c, 0, 2 * n + h2:2 * n + h2 + 1])
                    last.then_inc(s_mi1, 1)
                else:
                    act.sem_inc(s_mi1, 1)
                if n == 0 and c:
                    root(c)
            root(4)
            act.wait_ge(s_cp, 1)
            for h2 in range(2):
                last = copy(CO[:, :, h2, :], PS[:, h2, 0:256].rearrange("p (n d) -> p n d", n=4))
            last.then_inc(s_cpe, 1)

        def ml_dve(dve, chain):
            v = nc.vector
            tt = v.tensor_tensor
            dve.wait_ge(s_soo, 32)
            v.memset(MP[:, 0:1], 0.0)
            v.memset(VA[:, :, :, DV:W129], 1.0)
            v.memset(EM, 1.0)
            v.memset(CS, 0.0)
            chain.link(v.memset(MST[:, 0, :], 0.0))
            v.memset(EM[:, 0:SEQ:P], 0.0)
            chain.link(v.memset(EM[:, SEQ:T:NS], 0.0))
            dve.wait_ge(s_lg, 3)
            chain.link(v.scalar_tensor_tensor(out=LF, in0=LF, scalar=0.0, in1=R1, op0=ALU.min, op1=ALU.subtract))
            chain.link(v.tensor_tensor_scan(BB, EM, LF, 0.0, ALU.mult, ALU.add))
            chain.link(v.tensor_tensor_scan(MS_[:, 0:SEQ], LF[:, 0:SEQ], IG[:, 0:SEQ], 0.0, ALU.add, ALU.max))
            dve.wait_ge(s_mst, 32)
            sample = lambda row: row[:, SEQ:T].rearrange("p (b s) -> p b s", b=NB)
            for s in range(NS):
                prev = MP[:, 4:12] if s == 0 else sample(MS_)[:, :, s - 1]
                chain.link(tt(sample(MS_)[:, :, s], prev, sample(LF)[:, :, s], ALU.add))
                chain.link(tt(sample(MS_)[:, :, s], sample(MS_)[:, :, s], sample(IG)[:, :, s], ALU.max))
            v.tensor_copy(MP[:, 1:4], MS_[:, P - 1:SEQ - 1:P])
            tt(R1, BB, MS_, ALU.subtract)
            chain.link(tt(C1, IG, BB, ALU.subtract))
            tiles = lambda row: row[:, 0:SEQ].rearrange("p (c t) -> p c t", c=4)
            v.tensor_copy(DC[:, 0:4], R1[:, P - 1:SEQ:P])
            chain.link(v.tensor_copy(DC[:, 4:12], R1[:, SEQ + NS - 1:T:NS]))
            for view, a_, b_, n, w in ((tiles, 0, 4, 4, P), (sample, 4, 12, NB, NS)):
                tt(view(WI), view(R1), MP[:, a_:b_].unsqueeze(2).to_broadcast([MLH, n, w]), ALU.add)
                chain.link(tt(view(LF), view(C1), DC[:, a_:b_].unsqueeze(2).to_broadcast([MLH, n, w]), ALU.add))
            tt(DC, DC, MP, ALU.add).then_inc(s_row, 1)
            for m in range(10):
                pr, i = divmod(m, 5)
                rows = TILES[i][1]
                dve.wait_ge(s_mm, M_MV + m + 1)
                v.tensor_copy(VA[0:rows, i, 4 * pr:4 * pr + 4, 0:DV],
                              PS[0:rows, m % 4, :].rearrange("p (h v) -> p h v", h=4)).then_inc(s_ve, 1)
            dve.wait_ge(s_rowe, 4)
            tt(DD, DC.unsqueeze(1).to_broadcast([MLH, MLH, 12]),
               ident[0:8, 0:8].unsqueeze(2).to_broadcast([MLH, MLH, 12]), ALU.mult).then_inc(s_cst2, 1)
            dve.wait_ge(s_tkm, 1)
            v.tensor_copy(TK[:, 0:4].rearrange("p i q h -> p (i q h)"), PS[:, 0, 0:96])
            v.tensor_copy(TK[0:SMP, 4].rearrange("p q h -> p (q h)"), PS[0:SMP, 0, 96:120])
            v.tensor_copy(DCB.rearrange("p h g -> p (h g)"), PS[:, 1, 0:96])
            v.tensor_copy(DCT, PS[0:NB, 1, 128:136]).then_inc(s_tkv, 1)
            dve.wait_ge(s_tkv, 1)
            dve.sem_inc(s_tkv, 1)
            for i, (t0, rows) in enumerate(TILES):
                dve.wait_ge(s_ktm, i + 1)
                tt(KW[0:rows, i], PS[0:rows, 2 + i % 2, :].rearrange("p (h d) -> p h d", h=MLH),
                   TK[0:rows, i, 2, :].unsqueeze(2).to_broadcast([rows, MLH, DQK]), ALU.mult).then_inc(s_kwv, 1)
            dve.wait_ge(s_mm, M_MOG + 8)
            chain.link(v.memset(QX, 0.0))
            dve.wait_ge(s_qke, 8)
            for q in range(4):
                for b2 in range(2):
                    for h2 in range(2):
                        c0 = 8 * q + 4 * b2
                        last = v.tensor_copy(QX[64 * b2:64 * b2 + 64, h2:8:2, q, c0:c0 + 4],
                                             QM[64 * h2:64 * h2 + 64, :, SEQ + c0:SEQ + c0 + 4])
            last.then_inc(s_qx, 1)
            dve.wait_ge(s_ma, 1)
            tt(EXS, PS[0:SMP, 4, 0:256].rearrange("p (h t) -> p h t", h=MLH),
               const("s_causal").unsqueeze(1).to_broadcast([SMP, MLH, SMP]), ALU.add).then_inc(s_md1, 1)
            dve.wait_ge(s_kwv, 5)
            dve.wait_ge(s_c0, 16 * (MLH + 5))
            own = const("s_own").unsqueeze(2).to_broadcast([SMP, NB, DQK])

            def spread(h):
                if h >= 2:
                    dve.wait_ge(s_cu, h - 1)
                tt(KB[0:SMP, h % 2], KW[0:SMP, 4, h, :].unsqueeze(1).to_broadcast([SMP, NB, DQK]), own, ALU.mult)\
                    .then_inc(s_kb, 1)

            dve.wait_ge(s_mex, 1)
            for h2 in range(2):
                last = tt(SMS[:, h2:8:2, :], EXS[:, h2:8:2, :],
                          PS[0:SMP, 4 + h2, 256:384].rearrange("p (h t) -> p h t", h=4), ALU.mult)
            last.then_inc(s_md2, 1)
            dve.wait_ge(s_mit, 1)
            dve.wait_ge(s_mi1, 1)
            for h, (bank, j) in enumerate(INTRA):
                last = tt(NUM[0:SMP, 0, h, :], NUM[0:SMP, 0, h, :], PS[0:SMP, bank, j * W129:(j + 1) * W129], ALU.add)
            last.then_inc(s_md3, 1)
            dve.wait_ge(s_md3, 1)
            spread(0)
            spread(1)

            def norm_heads(j):
                i = 4 if j == 0 else j - 1
                rows = TILES[i][1]
                num = NUM[0:rows, j % 2]
                st = MST[0:rows]
                chain.link(v.scalar_tensor_tensor(out=st[:, 0, :], in0=num[:, :, DV], scalar=-1.0,
                                                  in1=num[:, :, DV], op0=ALU.mult, op1=ALU.max))
                tt(st[:, 0, :], st[:, 0, :], TK[0:rows, i, 1, :], ALU.max)
                for h in range(MLH):
                    last = v.tensor_tensor_reduce(out=SQH[0:rows, h, :], in0=num[:, h, 0:DV], in1=num[:, h, 0:DV],
                                                  scale=1.0, scalar=0.0, op0=ALU.mult, op1=ALU.add,
                                                  accum_out=st[:, 1, h:h + 1])
                chain.link(last)
                chain.link(v.reciprocal(st[:, 2, :], st[:, 0, :]))
                chain.link(tt(st[:, 3, :], st[:, 1, :], st[:, 2, :], ALU.mult))
                tt(st[:, 3, :], st[:, 3, :], st[:, 2, :], ALU.mult).then_inc(s_ms, 1)
                dve.wait_ge(s_mrt, j + 1)
                chain.link(v.reciprocal(st[:, 5, :], st[:, 4, :]))
                chain.link(tt(st[:, 6, :], st[:, 5, :], st[:, 2, :], ALU.mult))
                tt(num[:, :, 0:DV], num[:, :, 0:DV], st[:, 6, :].unsqueeze(2).to_broadcast([rows, MLH, DV]), ALU.mult)\
                    .then_inc(s_hv, 1)

            def gated(j):
                i = 4 if j == 0 else j - 1
                t0, rows = TILES[i]
                dve.wait_ge(s_mt, j + 1)
                for h in range(MLH):
                    v.scalar_tensor_tensor(out=OT[:, h, t0:t0 + rows],
                                           in0=PS[:, 6 + h // 4, (h % 4) * P:(h % 4) * P + rows],
                                           scalar=HN[:, h:h + 1], in1=OS[:, h, t0:t0 + rows],
                                           op0=ALU.mult, op1=ALU.mult).then_inc(s_mo, 1)

            norm_heads(0)
            for h in range(MLH):
                chain.link(tt(C0[:, h], C0[:, h], DCB[:, h, 4:12].unsqueeze(2).to_broadcast([P, NB, DQK]), ALU.mult))
                dve.wait_ge(s_cu, h + 1)
                tt(C0[:, h], C0[:, h], PS[:, h % 2, :].rearrange("p (b d) -> p b d", b=NB), ALU.add).then_inc(s_cn, 1)
                if h + 2 < MLH:
                    spread(h + 2)
            chain.link(tt(N0, N0, DCT.unsqueeze(2).to_broadcast([NB, MLH, DQK]), ALU.mult))
            dve.wait_ge(s_nu, 1)
            tt(N0, N0, PS[0:NB, 2, :].rearrange("p (h d) -> p h d", h=MLH), ALU.add).then_inc(s_nn, 1)
            gated(0)

            def add_intra(u):
                c, n = divmod(u, 4)
                dve.wait_ge(s_mit, u + 2)
                dve.wait_ge(s_mi1, u + 2)
                if n == 0:
                    dve.wait_ge(s_mt, c)
                num = NUM[:, (c + 1) % 2, 2 * n:2 * n + 2, :]
                ps = PS[:, 4 + u % 2, 0:2 * W129].rearrange("p (h v) -> p h v", h=2)
                if c:
                    tt(num, num, ps, ALU.add).then_inc(s_md3, 1)
                else:
                    v.tensor_copy(num, ps).then_inc(s_md3, 1)
                if n == 3:
                    dve.wait_ge(s_md3, u + 2)
                    norm_heads(c + 1)

            causal = const("causal").unsqueeze(1).to_broadcast([P, 2, P])
            for u in range(16):
                c, n = divmod(u, 4)
                dve.wait_ge(s_ma, u + 2)
                tt(EX[:, u % 2], PS[:, u % 2, 0:256].rearrange("p (h t) -> p h t", h=2), causal, ALU.add)\
                    .then_inc(s_md1, 1)
                dve.wait_ge(s_min, u + 2)
                if c:
                    dve.wait_ge(s_md4, u - 3)
                for h2 in range(2):
                    rows = slice(64 * h2, 64 * h2 + 64)
                    ps = PS[rows, 2 + u % 2, 260:260 + W129]
                    if c:
                        last = v.scalar_tensor_tensor(out=CS[rows, n, h2, :], in0=CS[rows, n, h2, :],
                                                      scalar=DCB[rows, 2 * n + h2, c:c + 1], in1=ps,
                                                      op0=ALU.mult, op1=ALU.add)
                    else:
                        last = v.tensor_copy(CS[rows, n, h2, :], ps)
                last.then_inc(s_md4, 1)
                dve.wait_ge(s_mex, u + 2)
                if u >= 2:
                    dve.wait_ge(s_mit, u)
                tt(SM[:, u % 2, 0], EX[:, u % 2, 0], PS[:, u % 2, 256:384], ALU.mult)
                tt(SM[:, u % 2, 1], EX[:, u % 2, 1], PS[:, 4 + u % 2, 384:512], ALU.mult).then_inc(s_md2, 1)
                if u >= 1:
                    add_intra(u - 1)
                if n == 2 and c:
                    gated(c)
            add_intra(15)
            gated(4)

        def ml_pool(pool):
            g = nc.gpsimd
            pool.wait_ge(s_row, 1)
            for w in range(17):
                if w >= 2:
                    pool.wait_ge(s_ma, w - 1)
                if w == 0:
                    n, t0, hs = SMP, SEQ, slice(0, 8)
                else:
                    c, hp = divmod(w - 1, 4)
                    n, t0, hs = P, c * P, slice(2 * hp, 2 * hp + 2)
                k = 8 if w == 0 else 2
                g.tensor_tensor(RD[:, w % 2, :].rearrange("p (h t) -> p h t", h=k),
                                R1[:, t0:t0 + n].unsqueeze(1).to_broadcast([MLH, k, n]),
                                ident[0:8, hs].unsqueeze(2).to_broadcast([MLH, k, n]), ALU.mult).then_inc(s_rd, 1)
                if w == 1:
                    with nc.allow_non_contiguous_dma(reason="72 maxima change places"):
                        pool.dma_start(O["mlstm_m_sample"][0].rearrange("b h -> h b"), MS_[:, SEQ + NS - 1:T:NS])\
                            .then_inc(s_mlo, 16)
                        pool.dma_start(O["mlstm_m_prompt"][0].rearrange("b h -> h b"), MS_[:, SEQ - 1:SEQ])\
                            .then_inc(s_mlo, 16)
                    for h in range(MLH):
                        pool.wait_ge(s_cn, h + 1)
                        pool.dma_start(O["mlstm_C_sample"][0, :, h].rearrange("b v d -> v b d"), C0[:, h])\
                            .then_inc(s_cso, 16)
                    pool.wait_ge(s_nn, 1)
                    pool.dma_start(O["mlstm_n_sample"][0].rearrange("b h d -> b (h d)"),
                                   N0.rearrange("b h d -> b (h d)")).then_inc(s_cso, 16)
            pool.wait_ge(s_md4, 16)
            with nc.allow_non_contiguous_dma(reason="512 sums change places"):
                for h2 in range(2):
                    pool.dma_start(O["mlstm_n_prompt"][0, 0].rearrange("(n h) d -> h d n", h=2)[h2],
                                   CS[64 * h2:64 * h2 + 64, :, h2, DV]).then_inc(s_mlo, 16)
            pool.wait_ge(s_cpe, 1)
            pool.dma_start(O["mlstm_C_prompt"][0, 0].rearrange("(n h) v d -> v n h d", h=2)
                           .rearrange("v n h d -> v (n h) d"),
                           CO.rearrange("p n h d -> p (n h) d")).then_inc(s_mlo, 16)
            pool.wait_ge(s_mlo, 80)

        block = ctx.enter_context(nc.Block())

        w_in = A["w_nsa_in"][0].rearrange("(k p) c -> p k c", p=P)
        w_out_rows = A["w_nsa_out"][0].rearrange("(g h d) c -> g h d c", g=GROUPS, h=HPG)
        w_up = [A["w_ffn_up"][i].rearrange("(k p) c -> p k c", p=P) for i in range(DEPTH)]
        w_dn = [A["w_ffn_down"][i].rearrange("(g k p) c -> g p k c", p=P, k=KT) for i in range(DEPTH)]
        w_ml = A["w_ml_in"][0].rearrange("(k p) c -> p k c", p=P)
        w_mo = A["w_ml_out"][0].rearrange("(k p) c -> p k c", p=P)

        def halves(ap, n=T):
            return ap.rearrange("p (h c) -> p h c", h=2)

        @block.sync
        def _(sp):
            def slot(k, src):
                r = k % RING
                if k >= RING:
                    sp.wait_ge(s_mm, freed(k - RING))
                sp.dma_start(R[:, r], src).then_inc(s_w[r], 16)

            sp.dma_start(XR[:, 0:4, :], A["x_prompt"][0].rearrange("(i p) c -> p i c", p=P)).then_inc(s_x, 16)
            sp.dma_start(XR[0:SMP, 4, :], A["x_sample"].rearrange("b t c -> (b t) c")).then_inc(s_x, 16)
            sp.dma_start(CONST[:, :], A["const"]).then_inc(s_x, 16)
            sp.dma_start(RNG[0:64, :], A["norm_g"].rearrange("l n (k p) -> (l n k) p", p=P)).then_inc(s_par, 16)
            sp.dma_start(RHN[0:8, :], A["ml_head_norm"].rearrange("l (k p) -> (l k) p", p=P)).then_inc(s_par, 16)
            for c in range(2):
                sp.dma_start(RPOS[0:16, c * P:(c + 1) * P].rearrange("a (l d) -> a l d", l=2),
                             A["cmp_pos"].rearrange("n (a l) c d -> c (n a) l d", l=2)[c]).then_inc(s_par, 16)
            sp.dma_start(RCW[:, :, :], A["ffn_conv_w"].rearrange("l j (c q) -> (l j c) q", q=P)
                         .rearrange("(i p) q -> p i q", p=P)).then_inc(s_par, 16)
            sp.dma_start(RCB[:, :], A["ffn_conv_b"].rearrange("l (c q) -> (l c) q", q=P)).then_inc(s_par, 16)
            for n in range(8):
                gp, h = divmod(n, HPG)
                for g2 in range(2):
                    c0, w0 = (n % 2) * P + g2 * HD, ((2 * gp + g2) * HPG + h) * HD
                    sp.dma_start(R[:, n // 2, :, c0:c0 + HD], w_in[:, :, w0:w0 + HD]).then_inc(s_w[n // 2], 16)
            sp.dma_start(WG[:, :, 0:48], w_in[:, :, 2560:2608]).then_inc(s_wg, 16)
            sp.dma_start(WG[:, :, 48:64], w_ml[:, :, 3072:3088]).then_inc(s_wg, 16)
            sp.dma_start(PT_I[0:1, :], A["page_table"].rearrange("b p -> (b p)").rearrange("(a n) -> a n", a=1))\
                .then_inc(s_pt, 16)
            sp.wait_ge(s_xe, 12)
            for c in range(2):
                for r in range(2):
                    sp.dma_start(W1[:, c, :, r * HD:(r + 1) * HD],
                                 A["w_cmp1"][0, c].rearrange("(r a l) d h -> r (l d) a h", r=2, l=2)[r])\
                        .then_inc(s_w1, 16)
                sp.dma_start(W2[0:HD, c, :], A["w_cmp2"][0, c]).then_inc(s_w1, 16)
            for k in range(6):
                slot(W_KV + k, w_in[:, :, (4 + k) * 256:(5 + k) * 256])
            nsa_loads(sp)
            for k in range(4):
                kk = W_AO + k
                sp.wait_ge(s_mm, freed(kk - RING))
                sp.wait_ge(s_spv, NB + 2)
                for gp in range(2):
                    for g2 in range(2):
                        sp.dma_start(R[64 * g2:64 * g2 + 64, kk % RING, 4 * gp:4 * gp + 4, :],
                                     w_out_rows[2 * gp + g2, :, :, k * 256:(k + 1) * 256].rearrange("h d c -> d h c"))\
                            .then_inc(s_w[kk % RING], 16)

            def ffn_loads(l):
                sp.wait_ge(s_ss, 3 + 4 * l)
                sp.dma_start(SI, A["state_ffn_conv"][l].rearrange("b r c -> (b r) c")).then_inc(s_sil, 16)
                with sp.Fori(0, 8) as i:
                    for j in range(4):
                        k0 = W_UP[l] + j
                        sp.wait_ge(s_mm, i * 8 + (M_UP[l] - 8 + (3, 4, 7, 8)[j]))
                        col = i * 512 + ((j // 2) * 256 + (j % 2) * FF)
                        sp.dma_start(R[:, k0 % RING], w_up[l][:, :, bass.ds(col, 256)]).then_inc(s_w[k0 % RING], 16)
                with sp.Fori(0, 4) as i:
                    for j in range(4):
                        k0 = W_DN[l] + j
                        sp.wait_ge(s_mm, i * 4 + (M_DN[l] - 3 + j))
                        sp.dma_start(R[:, k0 % RING], w_dn[l][j, :, :, bass.ds(i * 256, 256)])\
                            .then_inc(s_w[k0 % RING], 16)

            ffn_loads(0)
            ml_loads(sp, slot)
            for k in range(4):
                slot(W_MO + k, w_mo[:, :, k * 256:(k + 1) * 256])
            ffn_loads(1)

        @block.tensor
        def _(pe):
            mm, tr = nc.tensor.matmul, nc.tensor.transpose

            def arrived(k):
                pe.wait_ge(s_w[k % RING], loaded(k))

            def setup():
                pe.wait_ge(s_x, 48)
                for g in range(10):
                    i, hf = divmod(g, 2)
                    if g >= 8:
                        pe.wait_ge(s_xe, g - 7)
                    rows = TILES[i][1]
                    for q in range(4):
                        k = 4 * hf + q
                        last = tr(PS[:, g % 8, q * 128:q * 128 + rows], XR[0:rows, i, k * P:(k + 1) * P],
                                  ident[0:rows, 0:rows])
                    last.then_inc(s_xp, 1)
                pe.wait_ge(s_par, 96)
                pe.wait_ge(s_xe, 3)
                tr(PS[:, 2, 0:64], RNG[0:64, :], ident[0:64, 0:64])
                tr(PS[:, 2, 64:72], RHN[0:8, :], ident[0:8, 0:8])
                for c in range(2):
                    last = tr(PS[:, 2, 72 + 16 * c:88 + 16 * c],
                              RPOS[0:16, c * P:(c + 1) * P], ident[0:16, 0:16])
                last.then_inc(s_xp, 1)
                pe.wait_ge(s_xe, 4)
                for q in range(3):
                    tr(PS[:, 3, q * 128:(q + 1) * 128], RCW[:, q, :], ident)
                tr(PS[:, 3, 384:512], RCB[:, :], ident).then_inc(s_xp, 1)

            def norm_sum(idx):
                if idx == 0:
                    pe.wait_ge(s_cst, 1)
                    pe.wait_ge(s_xe, 12)
                gathered = idx % 2 == 1
                if gathered:
                    pe.wait_ge(s_gth, (idx + 1) // 2)
                for c in range(1 if gathered else 4):
                    if not gathered:
                        pe.wait_ge(s_sq, 4 * idx + c + 1)
                    for k in (2 * c, 2 * c + 1):
                        for hf in range(2):
                            last = mm(PS[:, hf, 0:HALF], ones[:, :], SQ[:, k, hf * HALF:(hf + 1) * HALF],
                                      start=(k == 0), stop=(k == (1 if gathered else KT - 1)))
                last.then_inc(s_ss, 1)

            def chunk(bank, lhs, src, normed=None):
                for k in range(KT):
                    if normed is not None:
                        pe.wait_ge(s_nrm, normed + k + 1)
                    for hf in range(2):
                        last = mm(PS[:, bank + hf, 0:HALF], lhs(k), src[:, k, hf * HALF:(hf + 1) * HALF],
                                  start=(k == 0), stop=(k == KT - 1))
                return last

            def project():
                for n in range(8):
                    gp, h = divmod(n, 4)
                    if n % 2 == 0:
                        arrived(n // 2)
                    if n >= 4:
                        pe.wait_ge(s_qe, n - 3)
                    chunk(2 * (n % 4), lambda k: R[:, n // 2, k, (n % 2) * P:(n % 2 + 1) * P], HT,
                          0 if n == 0 else None).then_inc(s_mm, 1)
                pe.wait_ge(s_qe, 8)
                m = 0
                for pr in range(3):
                    for s in range(2):
                        arrived(W_KV + 2 * pr + s)
                    r0 = (W_KV + 2 * pr) % RING
                    for i, (t0, rows) in enumerate(TILES):
                        if m >= 8:
                            pe.wait_ge(s_kve, m - 7)
                        for k in range(KT):
                            last = mm(PS[0:rows, m % 8, :], HT[:, k, t0:t0 + rows], R[:, r0:r0 + 2, k, :],
                                      start=(k == 0), stop=(k == KT - 1))
                        last.then_inc(s_mm, 1)
                        m += 1
                pe.wait_ge(s_wg, 32)
                for i, (t0, rows) in enumerate(TILES):
                    pe.wait_ge(s_kve, m - 7)
                    for k in range(KT):
                        last = mm(PS[0:rows, m % 8, 0:48], HT[:, k, t0:t0 + rows], WG[:, k, 0:48],
                                  start=(k == 0), stop=(k == KT - 1))
                    last.then_inc(s_mm, 1)
                    m += 1
                pe.wait_ge(s_kve, 15)
                pe.wait_ge(s_ge, 5)
                for br in range(2):
                    for gp in range(2):
                        for i in range(4):
                            last = tr(PS[:, m % 8, i * P:(i + 1) * P],
                                      KVP[:, i, 512 * (br + 1) + gp * P:512 * (br + 1) + (gp + 1) * P], ident)
                        last.then_inc(s_tk, 1)
                        m += 1
                for br in range(2):
                    for gp in range(2):
                        q = 2 * br + gp
                        last = tr(PS[:, m % 8, q * SMP:(q + 1) * SMP],
                                  KVS[0:SMP, 512 * (br + 1) + gp * P:512 * (br + 1) + (gp + 1) * P],
                                  ident[0:SMP, 0:SMP])
                last.then_inc(s_tk, 1)

            def out_product(w0, m0, z0, ready):
                for s, n in ready:
                    pe.wait_ge(s, n)
                for m in range(8):
                    if m % 2 == 0:
                        arrived(w0 + m // 2)
                    if m >= 4:
                        pe.wait_ge(s_z, z0 + m - 3)
                    r = (w0 + m // 2) % RING
                    chunk(2 * (m % 4), lambda k: R[:, r, k, (m % 2) * P:(m % 2 + 1) * P], OT).then_inc(s_mm, 1)

            def ffn(l):
                pe.wait_ge(s_sil, 16 * (l + 1))
                for g in range(2):
                    for c in range(32):
                        cc = 32 * g + c
                        last = tr(PS[:, 2 + g, c * 16:(c + 1) * 16], SI[:, cc * P:(cc + 1) * P], ident[0:16, 0:16])
                    last.then_inc(s_sip, 1)
                pe.wait_ge(s_sie, 2 * (l + 1))
                with pe.Fori(0, 8) as i:
                    for w in range(4):
                        pr, mc = divmod(w, 2)
                        for ag in range(2):
                            k0 = W_UP[l] + 2 * pr + ag
                            if mc == 0:
                                pe.wait_ge(s_w[k0 % RING], i * 16 + loaded(k0))
                            pe.wait_ge(s_ue, i * 8 + (2 * w + ag + 1 + 68 * l))
                            last = chunk(4 * mc + 2 * ag,
                                         lambda k: R[:, k0 % RING, k, mc * P:(mc + 1) * P], HT,
                                         8 * (2 + 4 * l) if w == 0 and ag == 0 else None)
                            last.then_inc(s_mm, 1)
                pe.wait_ge(s_y, 32 * (l + 1))
                pe.wait_ge(s_ue, 68 * l + 68)
                with pe.Fori(0, 2) as it:
                    for cp in range(2):
                        pe.wait_ge(s_z, it * 4 + (16 * l + 8 - 2 + 2 * cp))
                        for kg in range(4):
                            k0 = W_DN[l] + 4 * cp + kg
                            pe.wait_ge(s_w[k0 % RING], it * 32 + loaded(k0))
                            for mc in range(2):
                                for k in range(KT):
                                    for hf in range(2):
                                        last = mm(PS[:, 4 * cp + 2 * mc + hf, 0:HALF],
                                                  R[:, k0 % RING, k, mc * P:(mc + 1) * P],
                                                  YT[:, 8 * kg + k, hf * HALF:(hf + 1) * HALF],
                                                  start=(kg == 0 and k == 0), stop=(kg == 3 and k == KT - 1))
                            last.then_inc(s_mm, 1)

            def state_rows(l):
                pe.wait_ge(s_ul, 68 * (l + 1))
                for g in range(16):
                    if g >= 6:
                        pe.wait_ge(s_soe, 16 * l + g - 5)
                    for c in range(4):
                        last = tr(PS[0:18, 2 + g % 6, c * P:(c + 1) * P], UL[:, 4 * g + c, :], ident)
                    last.then_inc(s_sop, 1)

            def turn_back():
                pe.wait_ge(s_nrm, 60)
                pe.wait_ge(s_soe, 32)
                for g in range(10):
                    i, hf = divmod(g, 2)
                    if g == 1:
                        pe.wait_ge(s_nrm, 64)
                    t0, rows = TILES[i]
                    if g >= 8:
                        pe.wait_ge(s_fe, g - 7)
                    for q in range(4):
                        last = tr(PS[0:rows, g % 8, q * P:(q + 1) * P], XT[:, 4 * hf + q, t0:t0 + rows], ident)
                    last.then_inc(s_fp, 1)

            setup()
            norm_sum(0)
            project()
            nsa_pe(pe)
            out_product(W_AO, M_AO, 0, ((s_ot, 9), (s_ots, 16), (s_so, NB)))
            norm_sum(1)
            norm_sum(2)
            ffn(0)
            norm_sum(3)
            state_rows(0)
            norm_sum(4)
            ml_pe(pe)
            out_product(W_MO, M_MO, 16, ML_READY)
            norm_sum(5)
            norm_sum(6)
            ffn(1)
            norm_sum(7)
            state_rows(1)
            turn_back()

        @block.scalar
        def _(act):
            copy = nc.scalar.copy

            def squares(idx, src, waits=()):
                if idx:
                    act.wait_ge(s_ss, idx)
                for c in range(4):
                    for s, first, each in waits:
                        act.wait_ge(s, first + each * (c + 1))
                    nc.scalar.activation(SQ[:, 2 * c:2 * c + 2, :], src[:, 2 * c:2 * c + 2, :], ACT.Square)\
                        .then_inc(s_sq, 1)

            def root(idx):
                act.wait_ge(s_ss, idx + 1)
                if idx:
                    act.wait_ge(s_nrm, 8 * idx)
                nc.scalar.activation(halves(RT[:, :]), PS[:, 0:2, 0:HALF], ACT.Sqrt, bias=eps[:, 0:1],
                                     scale=1.0 / D).then_inc(s_rt, 1)

            def project():
                for n in range(8):
                    act.wait_ge(s_mm, M_Q + n + 1)
                    if n == 0:
                        act.wait_ge(s_xe, 12)
                    nc.scalar.activation(halves(QT[:, n, :]), PS[:, 2 * (n % 4):2 * (n % 4) + 2, 0:HALF], ACT.Copy,
                                         scale=HD ** -0.5).then_inc(s_qe, 1)
                for i, (t0, rows) in enumerate(TILES):
                    act.wait_ge(s_mm, M_GATE + i + 1)
                    nc.scalar.activation(G[0:rows, i, :], PS[0:rows, (15 + i) % 8, 0:48], ACT.Sigmoid).then_inc(s_ge, 1)

            def out_copies(m0):
                for m in range(8):
                    act.wait_ge(s_mm, m0 + m + 1)
                    copy(halves(ZT[:, m, :]), PS[:, 2 * (m % 4):2 * (m % 4) + 2, 0:HALF]).then_inc(s_z, 1)

            def ffn(l):
                for g in range(2):
                    act.wait_ge(s_sip, 2 * l + g + 1)
                    copy(UB[:, 32 * g:32 * (g + 1), :].rearrange("p c r -> p (c r)"), PS[:, 2 + g, :]).then_inc(s_sie, 1)
                with act.Fori(0, 8) as i:
                    for w in range(4):
                        mc = w % 2
                        for ag in range(2):
                            u = U[:, 2 * mc + ag, :]
                            act.wait_ge(s_mm, i * 8 + (M_UP[l] + 2 * w + ag + 1))
                            act.wait_ge(s_cvd, i * 8 + (2 * w + ag + 1 + 68 * l))
                            act.wait_ge(s_ul, i * 8 + (2 * w + ag + 1 + 68 * l))
                            bank = 4 * mc + 2 * ag
                            copy(u[:, 2:2 + HALF], PS[:, bank, 0:HALF])
                            copy(u[:, 2 + HALF:2 + SEQ], PS[:, bank + 1, 0:SEQ - HALF])
                            copy(u[:, 514:562].rearrange("p (b s) -> p b s", b=NB)[:, :, 2:6],
                                 PS[:, bank + 1, SEQ - HALF:HALF].rearrange("p (b s) -> p b s", b=NB))\
                                .then_inc(s_ue, 1)
                        act.wait_ge(s_cvd, i * 8 + (2 * w + 1 + 4 + 68 * l))
                        nc.scalar.activation(CV[:, 2 * mc, :], CV[:, 2 * mc, :], ACT.Gelu_apprx_tanh).then_inc(s_gel, 1)
                with act.Fori(0, 2) as it:
                    for cp in range(2):
                        act.wait_ge(s_mm, it * 8 + (M_DN[l] + 4 * cp + 4))
                        for mc in range(2):
                            bank = 4 * cp + 2 * mc
                            copy(halves(ZT[:, bass.ds(it * 4 + (2 * cp + mc), 1), :].rearrange("p a t -> p (a t)")),
                                 PS[:, bank:bank + 2, 0:HALF]).then_inc(s_z, 1)

            def state_rows(l):
                for g in range(16):
                    act.wait_ge(s_sop, 16 * l + g + 1)
                    copy(SO[:, g * 512:(g + 1) * 512], PS[0:18, 2 + g % 6, :]).then_inc(s_soe, 1)

            def turn_back():
                for g in range(10):
                    i, hf = divmod(g, 2)
                    rows = TILES[i][1]
                    act.wait_ge(s_fp, g + 1)
                    copy(YR[0:rows, i, hf * 512:(hf + 1) * 512], PS[0:rows, g % 8, :]).then_inc(s_fe, 1)

            act.wait_ge(s_cst, 1)
            act.wait_ge(s_xe, 12)
            squares(0, XT)
            root(0)
            project()
            nsa_act(act)
            out_copies(M_AO)
            squares(1, ZT, ((s_z, 0, 2),))
            root(1)
            squares(2, XT, ((s_nrm, 8, 2),))
            root(2)
            ffn(0)
            squares(3, ZT, ((s_z, 8, 2),))
            root(3)
            state_rows(0)
            squares(4, XT, ((s_nrm, 24, 2),))
            root(4)
            ml_act(act)
            out_copies(M_MO)
            act.wait_ge(s_z, 24)
            act.wait_ge(s_mlo, 80)
            squares(5, ZT)
            root(5)
            squares(6, XT, ((s_nrm, 40, 2),))
            root(6)
            ffn(1)
            squares(7, ZT, ((s_z, 24, 2),))
            root(7)
            state_rows(1)
            turn_back()

        @block.vector
        def _(dve):
            v = nc.vector
            chain = Chain(dve, s_dc)

            def setup():
                for g in range(10):
                    i, hf = divmod(g, 2)
                    t0, rows = TILES[i]
                    dve.wait_ge(s_xp, g + 1)
                    v.tensor_copy(XT[:, 4 * hf:4 * hf + 4, t0:t0 + rows],
                                  PS[:, g % 8, :].rearrange("p (k t) -> p k t", k=4)[:, :, 0:rows]).then_inc(s_xe, 1)
                dve.wait_ge(s_xp, 11)
                v.tensor_copy(NG[:, :], PS[:, 2, 0:64])
                v.tensor_copy(HN[:, :], PS[:, 2, 64:72])
                v.tensor_copy(POS[:, :], PS[:, 2, 72:104]).then_inc(s_xe, 1)
                dve.wait_ge(s_xp, 12)
                v.tensor_copy(CW[:, :], PS[:, 3, 0:384])
                v.tensor_copy(CB[:, :], PS[:, 3, 384:512]).then_inc(s_xe, 1)

            def scaled(idx, src, dst, add):
                if idx % 2 == 1:
                    for c in range(1, 4):
                        dve.wait_ge(s_sq, 4 * idx + c + 1)
                        ins = v.tensor_tensor(SQ[:, 0:2, :], SQ[:, 0:2, :], SQ[:, 2 * c:2 * c + 2, :], ALU.add)
                        if c < 3:
                            chain.link(ins)
                    ins.then_inc(s_gth, 1)
                dve.wait_ge(s_rt, idx + 1)
                chain.link(v.reciprocal(RR[:, :], RT[:, :]))
                if idx == 0:
                    dve.wait_ge(s_xe, 12)
                def join(k):
                    dve.wait_ge(s_dc, chain.k - done[0] + k + 1)
                    v.tensor_tensor(XT[:, k, :], XT[:, k, :], dst[:, k, :], ALU.add).then_inc(s_nrm, 1)

                done = [0]
                for k in range(KT):
                    g = NG[:, 8 * idx + k:8 * idx + k + 1]
                    ins = v.scalar_tensor_tensor(out=dst[:, k, :], in0=src[:, k, :], scalar=g, in1=RR[:, :],
                                                 op0=ALU.mult, op1=ALU.mult)
                    if add:
                        ins.then_inc(s_dc, 1)
                        chain.k += 1
                        done[0] += 1
                        if k:
                            join(k - 1)
                    else:
                        ins.then_inc(s_nrm, 1)
                if add:
                    join(KT - 1)

            def project():
                m = 0
                for pr in range(3):
                    for i, (t0, rows) in enumerate(TILES):
                        dve.wait_ge(s_mm, M_KV + m + 1)
                        dst = KVP[:, i, pr * 512:(pr + 1) * 512] if i < 4 else KVS[0:SMP, pr * 512:(pr + 1) * 512]
                        v.tensor_copy(dst, PS[0:rows, m % 8, :]).then_inc(s_kve, 1)
                        m += 1
                m = 20
                for q in range(4):
                    dve.wait_ge(s_tk, q + 1)
                    v.tensor_copy(KTS[:, q // 2, q % 2, 0:SEQ], PS[:, m % 8, :]).then_inc(s_tke, 1)
                    m += 1
                dve.wait_ge(s_tk, 5)
                v.tensor_copy(KTS[:, :, :, SEQ:T].rearrange("p r g t -> p (r g) t"),
                              PS[:, m % 8, 0:4 * SMP].rearrange("p (q t) -> p q t", q=4)).then_inc(s_tke, 1)

            def ffn(l):
                cw = CW[:, :].rearrange("p (l j c) -> p l j c", l=2, j=3)
                cb = CB[:, :].rearrange("p (l c) -> p l c", l=2)
                with dve.Fori(0, 8) as i:
                    fc = Chain(dve, s_cc, i * 16 + 128 * l)
                    for w in range(4):
                        mc = w % 2
                        for ag in range(2):
                            u, c = U[:, 2 * mc + ag, :], CV[:, 2 * mc + ag, :]
                            n = i * 4 + (w + 32 * ag)
                            dve.wait_ge(s_ue, i * 8 + (2 * w + ag + 1 + 4 + 68 * l))
                            dve.wait_ge(s_pad, i * 8 + (2 * w + ag + 1 + 64 * l))
                            fc.link(v.tensor_scalar(c, u[:, 2:562], cw[:, l, 2, bass.ds(n, 1)], cb[:, l, bass.ds(n, 1)],
                                                    ALU.mult, ALU.add))
                            fc.link(v.scalar_tensor_tensor(out=c, in0=u[:, 1:561], scalar=cw[:, l, 1, bass.ds(n, 1)],
                                                           in1=c, op0=ALU.mult, op1=ALU.add))
                            v.scalar_tensor_tensor(out=c, in0=u[:, 0:560], scalar=cw[:, l, 0, bass.ds(n, 1)],
                                                   in1=c, op0=ALU.mult, op1=ALU.add).then_inc(s_cvd, 1)
                        dve.wait_ge(s_cvd, i * 8 + (2 * w + 2 + 4 + 68 * l))
                        dve.wait_ge(s_gel, i * 4 + (w + 1 + 32 * l))
                        ca, cg = CV[:, 2 * mc, :], CV[:, 2 * mc + 1, :]
                        y = YT[:, bass.ds(i * 4 + w, 1), :].rearrange("p a t -> p (a t)")
                        v.tensor_tensor(y[:, 0:SEQ], ca[:, 0:SEQ], cg[:, 0:SEQ], ALU.mult)
                        v.tensor_tensor(y[:, SEQ:T].rearrange("p (b s) -> p b s", b=NB),
                                        ca[:, 512:560].rearrange("p (b s) -> p b s", b=NB)[:, :, 2:6],
                                        cg[:, 512:560].rearrange("p (b s) -> p b s", b=NB)[:, :, 2:6],
                                        ALU.mult).then_inc(s_y, 1)

            setup()
            scaled(0, XT, HT, False)
            project()
            nsa_dve(dve, chain)
            dve.wait_ge(s_kvo, 16 * (1 + 2 * NB))
            scaled(1, ZT, ZT, True)
            scaled(2, XT, HT, False)
            ffn(0)
            scaled(3, ZT, ZT, True)
            scaled(4, XT, HT, False)
            ml_dve(dve, chain)
            scaled(5, ZT, ZT, True)
            scaled(6, XT, HT, False)
            ffn(1)
            scaled(7, ZT, ZT, True)

        @block.gpsimd
        def _(pool):
            g = nc.gpsimd
            g.memset(ones[:, :], 1.0)
            g.memset(eps[:, :], EPS).then_inc(s_cst, 1)
            pool.wait_ge(s_xe, 12)
            g.memset(CJ[:, :, :], 0.0).then_inc(s_cjz, 1)
            pool.wait_ge(s_kve, 15)
            kvo = O["nsa_kv_prompt"].rearrange("n b s c g d -> (n b s) (c g d)").rearrange("(i p) c -> p i c", p=P)
            for c in range(2):
                pool.dma_start(kvo[:, :, c * 512:(c + 1) * 512], KVP[:, :, c * 512:(c + 1) * 512]).then_inc(s_kvp, 16)
            pool.dma_start(O["nsa_win_prompt"].rearrange("n b s c g d -> (n b s) (c g d)")
                           .rearrange("(i p) c -> p i c", p=P), KVP[:, :, 1024:1536]).then_inc(s_kvp, 16)
            pool.dma_start(O["nsa_kv_sample"].rearrange("n b s c g d -> (n b s) (c g d)"), KVS[0:SMP, 0:1024])\
                .then_inc(s_kvo, 16)
            wso = O["nsa_win_sample"].rearrange("n b s c g d -> (n b) s (c g d)")
            wsi = A["cache_nsa_win"].rearrange("n b s c g d -> (n b) s (c g d)")
            for b in range(NB):
                pool.dma_start(wso[b, WIN - NS:WIN, :], KVS[NS * b:NS * b + NS, 1024:1536]).then_inc(s_kvo, 16)
            pool.wait_ge(s_ge, 5)
            pool.dma_start(gsc[:, :], G[0:SMP, 4, :]).then_inc(s_gso, 16)
            pool.wait_ge(s_gso, 16)
            with nc.allow_non_contiguous_dma(reason="1536 gates change places"):
                for s in range(NS):
                    pool.dma_start(GS[HEADS * s:HEADS * (s + 1), :, :],
                                   gsc.rearrange("(b s) (h r) -> s h b r", s=NS, r=3)[s]).then_inc(s_gsi, 16)
            for b in range(NB):
                pool.dma_start(wso[b, 0:WIN - NS, :], wsi[b, NS:WIN, :]).then_inc(s_kvo, 16)

            def ffn(l):
                pool.wait_ge(s_nrm, 8 * (3 + 4 * l))
                g.memset(U[:, :, 0:2], 0.0).then_inc(s_ubw, 1)
                pool.wait_ge(s_ubw, l + 1)
                pool.sem_inc(s_ue, 4)
                pool.sem_inc(s_cvd, 4)
                pool.sem_inc(s_ul, 4)
                pool.wait_ge(s_sie, 2 * (l + 1))
                with pool.Fori(0, 8) as i:
                    for w in range(4):
                        mc = w % 2
                        for ag in range(2):
                            u = U[:, 2 * mc + ag, :]
                            n = i * 4 + (w + 32 * ag)
                            pool.wait_ge(s_cvd, i * 8 + (2 * w + ag + 1 + 68 * l))
                            g.tensor_copy(u[:, 514:562].rearrange("p (b s) -> p b s", b=NB)[:, :, 0:2],
                                          UB[:, bass.ds(n, 1), :].rearrange("p a (b r) -> p (a b) r", b=NB))\
                                .then_inc(s_pad, 1)
                            pool.wait_ge(s_ue, i * 8 + (2 * w + ag + 1 + 4 + 68 * l))
                            src = u[:, 512:512 + 48].rearrange("p (b s) -> p b s", b=8)
                            g.tensor_copy(UL[:, bass.ds(n, 1), 0:16].rearrange("p a (b r) -> p (a b) r", b=NB),
                                          src[:, :, 0:2])
                            g.tensor_copy(UL[:, bass.ds(n, 1), 16:18].rearrange("p a r -> p (a r)"), u[:, 560:562])\
                                .then_inc(s_ul, 1)
                pool.wait_ge(s_soe, 16 * (l + 1))
                so = O["ffn_conv_sample"][l].rearrange("b r c -> (b r) c")
                pool.dma_start(O["ffn_conv_prompt"][l, 0], SO[0:2, :]).then_inc(s_soo, 16)
                pool.dma_start(so, SO[2:18, :]).then_inc(s_soo, 16)

            ffn(0)
            pool.wait_ge(s_soo, 32)
            ml_pool(pool)
            ffn(1)
            pool.wait_ge(s_fe, 10)
            pool.dma_start(O["y_prompt"][0].rearrange("(i p) c -> p i c", p=P), YR[:, 0:4, :]).then_inc(s_fo, 16)
            pool.dma_start(O["y_sample"].rearrange("b s c -> (b s) c"), YR[0:SMP, 4, :]).then_inc(s_fo, 16)
            pool.wait_ge(s_fo, 32)
            pool.wait_ge(s_soo, 64)
            pool.wait_ge(s_kvp, 48)
            pool.wait_ge(s_kvo, 16 * (1 + 2 * NB))


INPUTS = ["x_prompt", "x_sample", "cache_nsa_kv", "cache_nsa_win", "state_mlstm_C", "state_mlstm_n", "state_mlstm_m",
          "state_ffn_conv", "page_table", "norm_g", "w_nsa_in", "w_nsa_out", "w_cmp1", "w_cmp2", "cmp_pos", "w_ml_in",
          "b_ml_gate", "ml_head_norm", "w_ml_out", "w_ffn_up", "ffn_conv_w", "ffn_conv_b", "w_ffn_down"]
OUTPUTS = [("y_prompt", (1, SEQ, D)), ("y_sample", (NB, NS, D)), ("nsa_kv_prompt", (1, 1, SEQ, 4, GROUPS, HD)),
           ("nsa_kv_sample", (1, NB, NS, 4, GROUPS, HD)), ("nsa_win_prompt", (1, 1, WIN, 2, GROUPS, HD)),
           ("nsa_win_sample", (1, NB, WIN, 2, GROUPS, HD)), ("mlstm_C_prompt", (1, 1, MLH, DV, DQK)),
           ("mlstm_C_sample", (1, NB, MLH, DV, DQK)), ("mlstm_n_prompt", (1, 1, MLH, DQK)),
           ("mlstm_n_sample", (1, NB, MLH, DQK)), ("mlstm_m_prompt", (1, 1, MLH)), ("mlstm_m_sample", (1, NB, MLH)),
           ("ffn_conv_prompt", (DEPTH, 1, 2, 2 * FF)), ("ffn_conv_sample", (DEPTH, NB, 2, 2 * FF))]


def kernel(**inputs):
    from concourse import bacc
    from concourse.bass_utils import run_bass_kernel_spmd

    nc = bacc.Bacc("TRN2", target_bir_lowering=False, num_devices=1)
    arrays = {f"in_{name}": np.ascontiguousarray(inputs[name]) for name in INPUTS}
    arrays["in_const"], at = tables()
    A = {name[3:]: nc.dram_tensor(name, a.shape, mybir.dt.from_np(a.dtype), kind="ExternalInput").ap()
         for name, a in arrays.items()}
    O = {name: nc.dram_tensor(f"out_{name}", shape, F32, kind="ExternalOutput").ap() for name, shape in OUTPUTS}
    trunk(nc, A, O, at, arrays["in_const"].shape[1])
    r = run_bass_kernel_spmd(nc, [arrays], core_ids=[0]).results[0]
    return tuple(r[f"out_{name}"] for name, _ in OUTPUTS)
```
